# Optimizing a Trainium2 kernel written in Bass

```python
import jax, jax.numpy as jnp
from jax import lax
import numpy as np

D_MODEL = 1024
BATCH = 1
SEQ = 256
DEPTH = 2

RET_HEADS = 4
RET_DH = 128
RET_W = RET_HEADS * RET_DH
CHUNK = 128
ROPE_BASE = 10000.0
POOL_WINDOWS = (2, 4, 8, 16)
POOL_GROUPS = 4
POOL_GW = 128
POOL_W = POOL_GROUPS * POOL_GW
RG_BLOCKS = 4
RG_BD = 128
RG_W = RG_BLOCKS * RG_BD
RG_CONV = 4
RG_C = 8.0
N_BRANCH = 3
SPLITS = (RET_W, RET_W, RET_W, RET_W, POOL_W, RG_W, RG_W, N_BRANCH * D_MODEL)
IN_W = sum(SPLITS)
N_EXPERTS = 64
N_GROUPS = 8
E_PER_GROUP = N_EXPERTS // N_GROUPS
TOPK_GROUPS = 4
TOP_K = 8
D_EXPERT = 256
ROUTED_SCALE = 2.5
EXPERT_BLOCK = 256
LN_EPS = 1e-5
GN_EPS = 1e-6
ALPHA = (2 * DEPTH) ** 0.25
BETA = (8 * DEPTH) ** -0.25

kernel_name = "hybrid_retention_pool_rglru_moe_deepnorm"

def layer_norm(x, g, b):
    xf = x.astype(jnp.float32)
    mu = xf.mean(-1, keepdims=True)
    var = jnp.square(xf - mu).mean(-1, keepdims=True)
    return ((xf - mu) * lax.rsqrt(var + LN_EPS) * g.astype(jnp.float32) + b.astype(jnp.float32)).astype(x.dtype)

def rope_tables(positions):
    half = RET_DH // 2
    inv = ROPE_BASE ** (-jnp.arange(half, dtype=jnp.float32) / half)
    ang = positions.astype(jnp.float32)[:, None] * inv[None, :]
    return jnp.cos(ang), jnp.sin(ang)

def apply_rope(t, cos, sin):
    half = RET_DH // 2
    t1, t2 = t[..., :half], t[..., half:]
    return jnp.concatenate([t1 * cos - t2 * sin, t1 * sin + t2 * cos], axis=-1)

def retention(q, k, v, g, cos, sin):
    B, S, _ = q.shape
    N = S // CHUNK
    f32 = jnp.float32

    def heads(t):
        return t.astype(f32).reshape(B, S, RET_HEADS, RET_DH).transpose(0, 2, 1, 3)

    qh = apply_rope(heads(q), cos, sin)
    kh = apply_rope(heads(k), cos, sin) * (RET_DH ** -0.5)
    vh = heads(v)
    qc = qh.reshape(B, RET_HEADS, N, CHUNK, RET_DH)
    kc = kh.reshape(B, RET_HEADS, N, CHUNK, RET_DH)
    vc = vh.reshape(B, RET_HEADS, N, CHUNK, RET_DH)

    log_g = jnp.log(1.0 - 2.0 ** (-5.0 - jnp.arange(RET_HEADS, dtype=f32)))
    idx = jnp.arange(CHUNK, dtype=f32)
    diff = idx[:, None] - idx[None, :]
    decay_mask = jnp.where(diff >= 0, jnp.exp(log_g[:, None, None] * jnp.maximum(diff, 0.0)), 0.0)

    scores = jnp.einsum('bhncd,bhnjd->bhncj', qc, kc) * decay_mask[None, :, None]
    o_intra = jnp.einsum('bhncj,bhnjd->bhncd', scores, vc)

    k_decay = jnp.exp(log_g[:, None] * (CHUNK - 1 - idx)[None, :])
    chunk_kv = jnp.einsum('bhncd,bhnce->bhnde', kc * k_decay[None, :, None, :, None], vc)
    chunk_decay = jnp.exp(log_g * CHUNK)[None, :, None, None]

    def step(state, kv):
        return state * chunk_decay + kv, state

    init = jnp.zeros((B, RET_HEADS, RET_DH, RET_DH), f32)
    _, prev = lax.scan(step, init, jnp.moveaxis(chunk_kv, 2, 0))
    prev = jnp.moveaxis(prev, 0, 2)
    q_decay = jnp.exp(log_g[:, None] * (idx + 1.0)[None, :])
    o_cross = jnp.einsum('bhncd,bhnde->bhnce', qc, prev) * q_decay[None, :, None, :, None]

    o = (o_intra + o_cross).reshape(B, RET_HEADS, S, RET_DH)
    mu = o.mean(-1, keepdims=True)
    var = jnp.square(o - mu).mean(-1, keepdims=True)
    o = (o - mu) * lax.rsqrt(var + GN_EPS)
    o = o.transpose(0, 2, 1, 3).reshape(B, S, RET_W)
    return (jax.nn.silu(g.astype(f32)) * o).astype(q.dtype)

def pool_branch(xp, pool_w, pool_scale):
    B, S, _ = xp.shape
    f32 = jnp.float32
    xg = xp.astype(f32).reshape(B, S, POOL_GROUPS, POOL_GW)
    cp = jnp.concatenate([jnp.zeros((B, 1, POOL_GROUPS, POOL_GW), f32), jnp.cumsum(xg, axis=1)], axis=1)
    t = jnp.arange(S)
    means = []
    for gi, w in enumerate(POOL_WINDOWS):
        n = jnp.minimum(w, t + 1)
        win = cp[:, 1:, gi] - jnp.take(cp[:, :, gi], t + 1 - n, axis=1)
        means.append(win / n.astype(f32)[None, :, None])
    pooled = jnp.stack(means, axis=2) - xg
    y = jnp.einsum('bsgc,gce->bsge', pooled, pool_w.astype(f32)).reshape(B, S, POOL_W)
    return (y * pool_scale.astype(f32)).astype(xp.dtype)

def _lin_comb(c1, c2):
    a1, b1 = c1
    a2, b2 = c2
    return a1 * a2, a2 * b1 + b2

def rglru_branch(xr, yr, conv_w, conv_b, wa, ba, wx, bx, lam):
    B, S, _ = xr.shape
    f32 = jnp.float32
    xf = xr.astype(f32)
    conv = conv_b.astype(f32)
    for k in range(RG_CONV):
        shifted = jnp.pad(xf, ((0, 0), (k, 0), (0, 0)))[:, :S]
        conv = conv + shifted * conv_w[k].astype(f32)
    cb = conv.reshape(B, S, RG_BLOCKS, RG_BD)
    r = jax.nn.sigmoid(jnp.einsum('bsnd,nde->bsne', cb, wa.astype(f32)).reshape(B, S, RG_W) + ba)
    i = jax.nn.sigmoid(jnp.einsum('bsnd,nde->bsne', cb, wx.astype(f32)).reshape(B, S, RG_W) + bx)
    log_a = RG_C * r * jax.nn.log_sigmoid(lam.astype(f32))
    a = jnp.exp(log_a)
    b = jnp.sqrt(-jnp.expm1(2.0 * log_a)) * (i * conv)
    _, h = lax.associative_scan(_lin_comb, (a, b), axis=1)
    return (h * jax.nn.gelu(yr.astype(f32))).astype(xr.dtype)

def token_mixer(x, cos, sin, w_in, gate_b, w_branch, w_out, pool_w, pool_scale,
                conv_w, conv_b, wa, ba, wx, bx, lam):
    B, S, D = x.shape
    h = x @ w_in
    cuts = list(np.cumsum(SPLITS)[:-1])
    q, k, v, g, xp, xr, yr, gl = jnp.split(h, cuts, axis=-1)
    branches = (
        retention(q, k, v, g, cos, sin),
        pool_branch(xp, pool_w, pool_scale),
        rglru_branch(xr, yr, conv_w, conv_b, wa, ba, wx, bx, lam),
    )
    gates = jax.nn.sigmoid((gl.reshape(B, S, N_BRANCH, D) + gate_b).astype(jnp.float32)).astype(x.dtype)
    merged = gates[:, :, 0] * (branches[0] @ w_branch[0])
    for bi in range(1, N_BRANCH):
        merged = merged + gates[:, :, bi] * (branches[bi] @ w_branch[bi])
    return merged @ w_out

def moe_ffn(x2, router_w, router_bias, w1, w3, w2, s_w1, s_w3, s_w2):
    T, D = x2.shape
    scores = jax.nn.sigmoid((x2 @ router_w).astype(jnp.float32))
    biased = scores + router_bias.astype(jnp.float32)
    grp_score = lax.top_k(biased.reshape(T, N_GROUPS, E_PER_GROUP), 2)[0].sum(-1)
    _, top_groups = lax.top_k(grp_score, TOPK_GROUPS)
    gmask = jnp.any(top_groups[:, :, None] == jnp.arange(N_GROUPS)[None, None, :], axis=1)
    masked = jnp.where(jnp.repeat(gmask, E_PER_GROUP, axis=1), biased, -jnp.inf)
    _, top_e = lax.top_k(masked, TOP_K)
    sel = jnp.take_along_axis(scores, top_e, axis=1)
    gate_w = sel / sel.sum(-1, keepdims=True) * ROUTED_SCALE

    A = T * TOP_K
    e_flat = top_e.reshape(A)
    tok_flat = jnp.arange(A, dtype=jnp.int32) // TOP_K
    w_flat = gate_w.reshape(A).astype(x2.dtype)
    order = jnp.argsort(e_flat)
    e_sorted = e_flat[order]
    counts = jnp.bincount(e_flat, length=N_EXPERTS)
    padded = ((counts + EXPERT_BLOCK - 1) // EXPERT_BLOCK) * EXPERT_BLOCK
    pad_end = jnp.cumsum(padded)
    pad_start = pad_end - padded
    start = jnp.cumsum(counts) - counts
    dest = pad_start[e_sorted] + (jnp.arange(A, dtype=jnp.int32) - start[e_sorted])
    P = A + N_EXPERTS * EXPERT_BLOCK
    n_blk = P // EXPERT_BLOCK
    buf_tok = jnp.full((P,), T, jnp.int32).at[dest].set(tok_flat[order])
    buf_w = jnp.zeros((P,), x2.dtype).at[dest].set(w_flat[order])
    blk_start = jnp.arange(n_blk, dtype=jnp.int32) * EXPERT_BLOCK
    blk_expert = jnp.minimum(jnp.searchsorted(pad_end, blk_start, side='right'), N_EXPERTS - 1)
    x_pad = jnp.concatenate([x2, jnp.zeros((1, D), x2.dtype)], axis=0)

    def run_block(args):
        e, tok, wt = args
        xb = x_pad[tok]
        hb = jax.nn.silu(xb @ w1[e]) * (xb @ w3[e])
        return (hb @ w2[e]) * wt[:, None]

    y = lax.map(run_block, (blk_expert, buf_tok.reshape(n_blk, EXPERT_BLOCK), buf_w.reshape(n_blk, EXPERT_BLOCK)))
    routed = jax.ops.segment_sum(y.reshape(P, D), buf_tok, num_segments=T + 1)[:T]
    shared = (jax.nn.silu(x2 @ s_w1) * (x2 @ s_w3)) @ s_w2
    return shared + routed

def setup_inputs(seed: int = 0) -> dict:
    key = jax.random.key(seed)
    ks = jax.random.split(key, 32)
    nrm = jax.random.normal
    L, D = DEPTH, D_MODEL
    f32 = jnp.float32
    a0 = jax.random.uniform(ks[14], (L, RG_W), f32, minval=0.9, maxval=0.999)
    s = a0 ** (1.0 / RG_C)
    return {
        "x": nrm(ks[0], (BATCH, SEQ, D), f32),
        "positions": jnp.arange(SEQ, dtype=jnp.int32),
        "w_in": nrm(ks[1], (L, D, IN_W), f32) * D ** -0.5,
        "gate_b": nrm(ks[2], (L, N_BRANCH, D), f32) * 0.1,
        "w_branch": nrm(ks[3], (L, N_BRANCH, RET_W, D), f32) * (RET_W ** -0.5) * BETA,
        "w_out": nrm(ks[4], (L, D, D), f32) * (D ** -0.5) * BETA,
        "pool_w": nrm(ks[5], (L, POOL_GROUPS, POOL_GW, POOL_GW), f32) * POOL_GW ** -0.5,
        "pool_scale": 1.0 + 0.1 * nrm(ks[6], (L, POOL_W), f32),
        "rg_conv_w": nrm(ks[7], (L, RG_CONV, RG_W), f32) * RG_CONV ** -0.5,
        "rg_conv_b": nrm(ks[8], (L, RG_W), f32) * 0.02,
        "rg_wa": nrm(ks[9], (L, RG_BLOCKS, RG_BD, RG_BD), f32) * RG_BD ** -0.5,
        "rg_ba": nrm(ks[10], (L, RG_W), f32) * 0.02,
        "rg_wx": nrm(ks[11], (L, RG_BLOCKS, RG_BD, RG_BD), f32) * RG_BD ** -0.5,
        "rg_bx": nrm(ks[12], (L, RG_W), f32) * 0.02,
        "rg_lambda": jnp.log(s) - jnp.log1p(-s),
        "ln1_g": 1.0 + 0.02 * nrm(ks[13], (L, D), f32),
        "ln1_b": 0.02 * nrm(ks[15], (L, D), f32),
        "router_w": nrm(ks[16], (L, D, N_EXPERTS), f32) * D ** -0.5,
        "router_bias": nrm(ks[17], (L, N_EXPERTS), f32) * 0.01,
        "exp_w1": nrm(ks[18], (L, N_EXPERTS, D, D_EXPERT), f32) * D ** -0.5,
        "exp_w3": nrm(ks[19], (L, N_EXPERTS, D, D_EXPERT), f32) * D ** -0.5,
        "exp_w2": nrm(ks[20], (L, N_EXPERTS, D_EXPERT, D), f32) * (D_EXPERT ** -0.5) * BETA,
        "sh_w1": nrm(ks[21], (L, D, D_EXPERT), f32) * D ** -0.5,
        "sh_w3": nrm(ks[22], (L, D, D_EXPERT), f32) * D ** -0.5,
        "sh_w2": nrm(ks[23], (L, D_EXPERT, D), f32) * (D_EXPERT ** -0.5) * BETA,
        "ln2_g": 1.0 + 0.02 * nrm(ks[24], (L, D), f32),
        "ln2_b": 0.02 * nrm(ks[25], (L, D), f32),
    }

def reference(x, positions, w_in, gate_b, w_branch, w_out, pool_w, pool_scale,
              rg_conv_w, rg_conv_b, rg_wa, rg_ba, rg_wx, rg_bx, rg_lambda,
              ln1_g, ln1_b, router_w, router_bias, exp_w1, exp_w3, exp_w2,
              sh_w1, sh_w3, sh_w2, ln2_g, ln2_b):
    B, S, D = x.shape
    cos, sin = rope_tables(positions)
    for l in range(DEPTH):
        m = token_mixer(x, cos, sin, w_in[l], gate_b[l], w_branch[l], w_out[l], pool_w[l], pool_scale[l],
                        rg_conv_w[l], rg_conv_b[l], rg_wa[l], rg_ba[l], rg_wx[l], rg_bx[l], rg_lambda[l])
        x = layer_norm(ALPHA * x + m, ln1_g[l], ln1_b[l])
        f = moe_ffn(x.reshape(B * S, D), router_w[l], router_bias[l], exp_w1[l], exp_w3[l], exp_w2[l],
                    sh_w1[l], sh_w3[l], sh_w2[l]).reshape(B, S, D)
        x = layer_norm(ALPHA * x + f, ln2_g[l], ln2_b[l])
    return x


_drawn_inputs = setup_inputs


def setup_inputs(seed=0):
    import zlib

    import numpy as np

    out = dict(_drawn_inputs(seed))
    spreads = {}
    factors = {'rg_ba': 59.872, 'rg_bx': 31.387}
    for name, (base, spread) in spreads.items():
        noise = np.random.default_rng([zlib.crc32(name.encode()), seed]).standard_normal(out[name].shape)
        drawn = base * np.exp(spread * noise) if base else spread * noise
        out[name] = __import__('jax').numpy.asarray(drawn.astype(out[name].dtype))
    for name, factor in factors.items():
        out[name] = (out[name] * factor).astype(out[name].dtype)
    return out
```

```python
from contextlib import ExitStack

import numpy as np

import concourse.bass as bass
from concourse import mybir

F32 = mybir.dt.float32
R32 = mybir.dt.float32r
I32 = mybir.dt.int32
ALU = mybir.AluOpType
ACT = mybir.ActivationFunctionType
AX = mybir.AxisListType

P = 128
DEPTH, S, D = 2, 256, 1024
T = S // P
KD = D // P
H = 4
BW = H * P
KB = BW // P
CW = 256
PB = 4
RING = 4
XP0, XR0, YR0 = 4 * BW, 5 * BW, 6 * BW
Q0C, K0C, V0C, G0C, GL0 = 0, BW, 2 * BW, 3 * BW, 7 * BW
N_E, FE = 64, 256
E_GROUPS, TOP_GROUPS, TOP_K = 8, 4, 8
CAP = 64
QUAD = 4
NQ = N_E // QUAD
MAX_ROUNDS = S // CAP
ROUTED_SCALE = 2.5
ALPHA = (2 * DEPTH) ** 0.25
LN_EPS, GN_EPS = 1e-5, 1e-6
RG_C = 8.0
FAR = 4096.0
BIG = 1e30

N_CHUNKS = 6 + 4 + 2 + 2 + 12 + 4
C_QK, C_V, C_G, C_GL, C_OUT = 6, 10, 12, 14, 26
N_PIECES = 72
P_QK, P_V, P_G, P_GL, P_OUT = 12, 20, 24, 28, 64

TAB = {}
_at = 0
for _name, _n in (("ident", P), ("before", P), ("ones", P), ("mean", P), ("lower", E_GROUPS * E_GROUPS), ("slot", CAP),
                  ("thresh", MAX_ROUNDS - 1), ("decay_in", H * P), ("decay_across", H * P), ("inv_n", H * S),
                  ("freq", 1), ("sign", 1)):
    TAB[_name] = (_at, _at + _n)
    _at += _n
TAB_W = _at
GB, CVW, CVB, BA, BX, LAM, PSC, SP8, NSP8, PAR_W = 0, 24, 40, 44, 48, 52, 56, 60, 64, 68
PAR_ROWS = 60


class Signal:

    def __init__(self, nc, ctx, name, n, credit=0):
        self.sem, self.n, self.credit = ctx.enter_context(nc.semaphore(name)), n, credit

    def __call__(self, layer, k):
        return layer * self.n + (k + self.credit)


def shape_tables():
    t = np.zeros((P, TAB_W), np.float64)
    i = np.arange(P)

    def put(name, a):
        t[:, TAB[name][0]:TAB[name][1]] = a

    put("ident", np.eye(P))
    put("before", i[:, None] < i[None, :])
    put("ones", 1.0)
    put("mean", 1.0 / P)
    g = np.arange(E_GROUPS)
    put("lower", (g[None, :] < g[:, None]).reshape(1, -1))
    put("slot", np.arange(CAP)[None, :] + FAR)
    put("thresh", CAP * np.arange(1, MAX_ROUNDS)[None, :])
    log_g = np.log(1.0 - 2.0 ** (-5.0 - np.arange(H)))
    ahead = i[None, :] - i[:, None]
    scale = P ** -0.5
    put("decay_in", np.concatenate([np.where(ahead >= 0, np.exp(lg * np.maximum(ahead, 0)), 0.0) * scale for lg in log_g], 1))
    put("decay_across", np.concatenate([np.exp(lg * (ahead + P)) * scale for lg in log_g], 1))
    put("inv_n", np.concatenate([1.0 / np.minimum(2 ** (h + 1), np.arange(S) + 1) for h in range(H)])[None, :])
    put("freq", (10000.0 ** (-(i % 64) / 64.0))[:, None])
    put("sign", np.where(i < 64, -1.0, 1.0)[:, None])
    return t.astype(np.float32)


def trunk(nc, x, positions, tables, w_in, gate_b, w_branch, w_out, pool_w, pool_scale, rg_conv_w, rg_conv_b,
          rg_wa, rg_ba, rg_wx, rg_bx, rg_lambda, ln1_g, ln1_b, router_w, router_bias, exp_w1, exp_w3, exp_w2,
          sh_w1, sh_w3, sh_w2, ln2_g, ln2_b, out):
    with ExitStack() as ctx:
        place = [(nc.sbuf_base + 31) // 32 * 32]

        def at(name, shape, dt, offset):
            return nc.alloc_sbuf_tensor_at(name, [P] + shape, dt, offset=offset)

        def keep(name, shape, dt=F32):
            t = at(name, shape, dt, place[0])
            place[0] += (int(np.prod(shape)) * 4 + 31) // 32 * 32
            return t

        w13 = [keep("w13_a", [2, 2, KD * FE]), None]
        raw = keep("raw", [RING, PB, CW])
        x_tok = keep("x_tok", [T, D])
        xs_hi = keep("xs_hi", [KD, S], R32)
        xs_lo = keep("xs_lo", [KD, S], R32)
        tab = keep("tab", [TAB_W])
        ln_place = place[0]
        lnp = keep("lnp", [2, D])
        small_w = at("small_w", [3, H, P], F32, ln_place)
        rw = keep("rw", [KD, N_E])
        par = keep("par", [DEPTH, PAR_W])
        parl = keep("parl", [PAR_W])
        rbias = keep("rbias", [DEPTH])
        rbl = keep("rbl", [1])
        rope_c = keep("rope_c", [S])
        rope_s = keep("rope_s", [S])
        stats = keep("stats", [T, 2, 6])
        mv = keep("mv", [T, 2])
        sd = keep("sd", [T])
        eps = keep("eps", [2])
        rounds_i = keep("rounds_i", [1], I32)

        r1 = place[0]
        w13[1] = keep("w13_b", [2, 2, KD * FE])
        UNIT = H * S * 4
        mix = at("mix", [6, 2 * S], F32, r1)
        xp, xr, yr = (mix[:, 2 * i:2 * i + 2].rearrange("p a (h s) -> p (a h) s", s=S) for i in range(3))
        decayed = at("decayed", [2, 512], F32, r1)
        gelu = at("gelu", [H, S], F32, r1 + UNIT)
        conv = at("conv", [H, S], F32, r1 + 3 * UNIT)
        hid = at("hid", [H, S], F32, r1 + 3 * UNIT)
        rg = at("rg", [H, S], F32, r1 + 4 * UNIT)
        ig = at("ig", [H, S], F32, r1 + 5 * UNIT)
        ag = at("ag", [H, S], F32, r1 + 6 * UNIT)
        pooled = at("pooled", [H, S], F32, r1 + 7 * UNIT)
        ret = at("ret", [2, 2 * S], F32, r1 + 7 * UNIT)
        shw = at("shw", [2, KD, FE], F32, r1)
        shw2 = at("shw2", [2, D], F32, r1 + 2 * KD * FE * 4)
        r2 = place[0]
        w2 = [keep("w2_a", [2, 2 * D]), keep("w2_b", [2, 2 * D])]
        whi = at("whi", [RING, PB, CW], R32, r2)
        wlo = at("wlo", [RING, PB, CW], R32, r2 + RING * PB * CW * 4)
        r3 = place[0]
        qk = keep("qk", [4, 2 * S])
        val = keep("val", [T, BW])
        gate_g = keep("gate_g", [2, 2 * S])
        pool_b = at("pool_b", [H, S], F32, place[0] - UNIT)
        merged = keep("merged", [4, 2 * S])
        recip_u = at("recip_u", [H, S], F32, place[0] - 2 * UNIT)
        br_hi = keep("br_hi", [2, KB, S], R32)
        br_lo = keep("br_lo", [2, KB, S], R32)
        tmp1 = keep("tmp1", [2 * S])
        tmp2 = keep("tmp2", [2 * S])
        sg = keep("sg", [2 * S])
        end_mixer = place[0]
        place[0] = r3
        xt = keep("xt", [KD, S])
        xg = keep("xg", [KD, QUAD * CAP])
        pick = keep("pick", [T, QUAD, CAP], R32)
        pick_w = keep("pick_w", [T, QUAD, CAP])
        pick_t = keep("pick_t", [2, S], R32)
        y_hi = keep("y_hi", [2, 512], R32)
        y_lo = keep("y_lo", [2, 512], R32)
        m_sg = keep("m_sg", [2, 2 * P])
        m_t = keep("m_t", [2, 2 * P])
        m_h = keep("m_h", [2, 2, P])
        m_ht = keep("m_ht", [2, 2, P])
        slot_gate = keep("slot_gate", [2])
        sc_t = keep("sc_t", [S])
        sc = keep("sc", [T, 2, N_E])
        g8 = keep("g8", [T, E_GROUPS, 8])
        grp = keep("grp", [T, E_GROUPS])
        cmp_a = keep("cmp_a", [T * E_GROUPS, E_GROUPS])
        cmp_b = keep("cmp_b", [T * E_GROUPS, E_GROUPS])
        gmask = keep("gmask", [T, E_GROUPS])
        gpen = keep("gpen", [T, E_GROUPS])
        masked = keep("masked", [T, N_E])
        best = keep("best", [T, 8])
        taken = keep("taken", [T, N_E])
        chosen = keep("chosen", [T, N_E])
        weight = keep("weight", [T, N_E])
        den = keep("den", [T])
        rank = keep("rank", [T, (MAX_ROUNDS * N_E + QUAD)])
        most = keep("most", [1])
        over = keep("over", [MAX_ROUNDS])
        shared_sg, shared_t = m_sg[:].rearrange("p a s -> p (a s)"), m_t[:].rearrange("p a s -> p (a s)")
        m_h_shared = m_h[:].rearrange("p a b s -> p (a b s)").rearrange("p (j s) -> p j s", j=2)
        assert max(end_mixer, place[0]) <= nc.sbuf_usable_end, (end_mixer, place[0], nc.sbuf_usable_end)
        rows = at("rows", [P], F32, r1)
        pos_i = at("pos_i", [S], I32, r1 + UNIT)
        ang = at("ang", [S], F32, r1 + 2 * UNIT)
        turns = at("turns", [2, S], F32, r1 + 3 * UNIT)
        lam_t = at("lam_t", [4, DEPTH, H], F32, r1 + 4 * UNIT)
        reduced = at("reduced", [2, S], F32, r1 + 5 * UNIT)

        bank = [ctx.enter_context(nc.psum_tensor(f"bank{i}", [P, 512], F32)) for i in range(8)]

        def tb(name):
            return tab[:, TAB[name][0]:TAB[name][1]]

        ident, ones = tb("ident"), tb("ones")

        def plain(name):
            return ctx.enter_context(nc.semaphore(name))

        def sig(name, n, credit=0):
            return Signal(nc, ctx, name, n, credit)

        start_in, rows_ps, start_dve, start_act = plain("start_in"), plain("rows_ps"), plain("start_dve"), plain("start_act")
        raw_in = [sig(f"raw_in{i}", 16 * N_PIECES // RING) for i in range(RING)]
        hi_done = sig("hi_done", N_PIECES)
        lo_even, lo_odd = sig("lo_even", N_PIECES // 2, 1), sig("lo_odd", N_PIECES // 2, 1)
        used = sig("used", N_PIECES, RING)
        evac = sig("evac", N_CHUNKS, 2)
        par_ready = sig("par_ready", 2)
        xt_ps, xs_hi_done, xs_lo_done = sig("xt_ps", 4), sig("xs_hi_done", 4), sig("xs_lo_done", 4)
        small_in, ln_in, rw_in = sig("small_in", 48), sig("ln_in", 64), sig("rw_in", 16)
        conv_done = sig("conv_done", 16)
        pool_sum = sig("pool_sum", 13)
        rope_m, roped = sig("rope_m", 8), sig("roped", 4, 1)
        ri_ps, r_done, i_done, a_done, u_done = sig("ri_ps", 2), sig("r_done", 4), sig("i_done", 4), sig("a_done", 4), sig("u_done", 4)
        lru, lru_root = sig("lru", 10), sig("lru_root", 1)
        gelu_sq, gelu_arg, gelu_cube, gelu_tanh, gelu_gate = (sig(n, 1) for n in ("gelu_sq", "gelu_arg", "gelu_cube", "gelu_tanh", "gelu_gate"))
        pl_ps, br_hi_done, br_ready = sig("pl_ps", 1), sig("br_hi_done", 6), sig("br_ready", 6)
        g_sg = sig("g_sg", 2)
        sc_ps, decayed_done, o_ps, o_sb, mean_ps = sig("sc_ps", 4), sig("decayed_done", 4), sig("o_ps", 2), sig("o_sb", 2), sig("mean_ps", 2)
        o_dev, o_sq, var_ps, o_sd, o_norm = sig("o_dev", 2), sig("o_sq", 2), sig("var_ps", 2), sig("o_sd", 2), sig("o_norm", 6)
        gates_sg, merge_done = sig("gates_sg", 24), sig("merge_done", 12)
        m_hi_done, m_lo_done = sig("m_hi_done", 4), sig("m_lo_done", 4)
        ln, ln_sd = sig("ln", 26, 1), sig("ln_sd", 2)
        xt2_ps, xt2_dve, xt2_act, tok_hi, tok_lo = sig("xt2_ps", 4), sig("xt2_dve", 2), sig("xt2_act", 2), sig("tok_hi", 2), sig("tok_lo", 2)
        logit_ps, sig_t, biased_t, sc_tok_ps = sig("logit_ps", 1, 1), sig("sig_t", 1), sig("biased_t", 1), sig("sc_tok_ps", 1)
        route, rank_ps = sig("route", 46), sig("rank_ps", 1)
        rounds_ready = sig("rounds_ready", 1)
        sh_in, sh_ps, sh_sg, sh_h, sh_done = sig("sh_in", 48), sig("sh_ps", 2), sig("sh_sg", 1), sig("sh_h", 2), sig("sh_done", 1)
        w13_in, w2_in = [plain("w13_in_a"), plain("w13_in_b")], [plain("w2_in_a"), plain("w2_in_b")]
        picked, picked_w, gathered = plain("picked"), plain("picked_w"), plain("gathered")
        xg_dve, xg_act = plain("xg_dve"), plain("xg_act")
        up_done = [plain("up_done_a"), plain("up_done_b")]
        pick_t_ps, pick_t_done = plain("pick_t_ps"), plain("pick_t_done")
        h_sg, h_t, h_done, ht_ps, ht_done = plain("h_sg"), plain("h_t"), plain("h_done"), plain("ht_ps"), plain("ht_done")
        y_ps, y_hi_done, y_lo_done, added = plain("y_ps"), plain("y_hi_done"), plain("y_lo_done"), plain("added")
        passed = {eng: plain(f"passed_{i}") for i, eng in enumerate((nc.sync, nc.tensor, nc.scalar, nc.gpsimd, nc.vector))}
        start_chain = sig("start_chain", 0)
        out_sem = plain("out_done")

        block = ctx.enter_context(nc.Block())

        def wait_alone(eng, signal, l, k):
            eng.wait_ge(signal.sem, signal(l, k))
            eng.sem_inc(passed[eng], 1)

        def lo_part(eng, vec, l, a, n=0, i=0):
            s = a % RING
            eng.wait_ge(hi_done.sem, hi_done(l, a + 1 + n * i))
            which = (lo_even, lo_odd)[a % 2]
            vec.tensor_tensor(wlo[:, s], raw[:, s], whi[:, s].bitcast(F32), ALU.subtract).then_inc(which.sem, 1)

        @block.sync
        def _(sp):
            sp.dma_start(x_tok[:], x.rearrange("b (t p) d -> p (b t) d", p=P)).then_inc(start_in, 16)
            sp.dma_start(tab[:], tables).then_inc(start_in, 16)
            with nc.allow_non_contiguous_dma(reason="one value per partition"):
                sp.dma_start(rbias[0:N_E, :], router_bias.rearrange("l e -> e l")).then_inc(start_in, 16)
            sp.dma_start(pos_i[:], positions.unsqueeze(0).to_broadcast([P, S])).then_inc(start_in, 16)
            for l in range(DEPTH):
                for at_row, src in ((GB, gate_b[l].rearrange("b (n c) -> (b n) c", c=P)),
                                    (CVW, rg_conv_w[l].rearrange("k (n c) -> (k n) c", c=P)),
                                    (CVB, rg_conv_b[l].rearrange("(n c) -> n c", c=P)),
                                    (BA, rg_ba[l].rearrange("(n c) -> n c", c=P)),
                                    (BX, rg_bx[l].rearrange("(n c) -> n c", c=P)),
                                    (LAM, rg_lambda[l].rearrange("(n c) -> n c", c=P)),
                                    (PSC, pool_scale[l].rearrange("(n c) -> n c", c=P))):
                    r = l * PAR_ROWS + at_row
                    sp.dma_start(rows[r:r + src.shape[0], :], src).then_inc(start_in, 16)

            def piece(l, source, a, n=0, i=0):
                s = a % RING
                which = (lo_even, lo_odd)[a % 2]
                if isinstance(n, int) and n == 0 and a < RING:
                    sp.wait_ge(which.sem, which(l, 0))
                else:
                    sp.wait_ge(which.sem, which(l, (a - RING) // 2 + 1 + (n // 2) * i))
                sp.dma_start(raw[:, s], source).then_inc(raw_in[s].sem, 16)

            def in_piece(l, col, half):
                return w_in[l].rearrange("(q k) c -> q k c", k=KD)[:, half * PB:(half + 1) * PB, bass.ds(col, CW)]

            quads = sp.alloc_register("quads_before")
            sp.reg_mov(quads, 0)
            with sp.Fori(0, DEPTH) as l:
                for a in range(RING):
                    piece(l, in_piece(l, XP0 + (a // 2) * CW, a % 2), a)
                sp.wait_ge(ln.sem, ln(l, 0))
                for j, w in enumerate((pool_w, rg_wa, rg_wx)):
                    sp.dma_start(small_w[:, j], w[l].rearrange("n c e -> c n e")).then_inc(small_in.sem, 16)
                sp.wait_ge(logit_ps.sem, logit_ps(l, 0))
                sp.dma_start(rw[:], router_w[l].rearrange("(q k) e -> q k e", k=KD)).then_inc(rw_in.sem, 16)
                for a in range(RING, P_QK):
                    piece(l, in_piece(l, XP0 + (a // 2) * CW, a % 2), a)
                q_first = sp.snap(quads)
                sp.wait_ge(up_done[0], q_first + 1)
                for m, w in enumerate((exp_w1, exp_w3)):
                    sp.dma_start(w13[0][:, m], w[l, 0:2].rearrange("e (q k) f -> q e (k f)", k=KD)).then_inc(w13_in[0], 16)
                with sp.Fori(0, 2) as i:
                    for u in range(4):
                        piece(l, in_piece(l, Q0C + (u // 2) * CW + 2 * CW * i, u % 2), P_QK + u, 4, i)
                for u in range(4):
                    piece(l, in_piece(l, V0C + (u // 2) * CW, u % 2), P_V + u)
                for u in range(4):
                    piece(l, in_piece(l, G0C + (u // 2) * CW, u % 2), P_G + u)
                sp.wait_ge(pl_ps.sem, pl_ps(l, 1))
                sp.wait_ge(ri_ps.sem, ri_ps(l, 2))
                sp.dma_start(lnp[:, 0], ln1_g[bass.ds(l, 1)].to_broadcast([P, D])).then_inc(ln_in.sem, 16)
                sp.dma_start(lnp[:, 1], ln1_b[bass.ds(l, 1)].to_broadcast([P, D])).then_inc(ln_in.sem, 16)

                def gl_pieces(j, b):
                    for v in range(4):
                        for half in range(2):
                            piece(l, in_piece(l, GL0 + v * CW + D * b, half), P_GL + 3 * v + half, 12, j)
                        piece(l, w_branch[l, b].rearrange("(k q) c -> q k c", q=P)[:, :, v * CW:(v + 1) * CW],
                              P_GL + 3 * v + 2, 12, j)

                gl_pieces(0, 1)
                with sp.Fori(1, 3) as j:
                    gl_pieces(j, (j + 1) % 3)
                sp.wait_ge(br_ready.sem, br_ready(l, 6))
                sp.wait_ge(up_done[1], q_first + 1)
                for j, w in enumerate((sh_w1, sh_w3)):
                    sp.dma_start(shw[:, j], w[l].rearrange("(q k) f -> q k f", k=KD)).then_inc(sh_in.sem, 16)
                sp.dma_start(shw2[:], sh_w2[l].rearrange("(j q) d -> q j d", q=P)).then_inc(sh_in.sem, 16)
                for a in range(8):
                    piece(l, w_out[l].rearrange("(k q) c -> q k c", q=P)[:, (a % 2) * PB:(a % 2 + 1) * PB,
                                                                       (a // 2) * CW:(a // 2 + 1) * CW], P_OUT + a)

                def up_load(X, e):
                    for m, w in enumerate((exp_w1, exp_w3)):
                        sp.dma_start(w13[X][:, m], w[l, bass.ds(e, 2)].rearrange("e (q k) f -> q e (k f)", k=KD)).then_inc(w13_in[X], 16)

                def down_load(X, e):
                    sp.dma_start(w2[X][:], exp_w2[l, bass.ds(e, 2)].rearrange("e (q j) d -> q e (j d)", j=2)).then_inc(w2_in[X], 16)

                sp.wait_ge(used.sem, used(l, N_PIECES))
                down_load(0, 0)
                down_load(1, 2)
                sp.wait_ge(ln.sem, ln(l, 13))
                sp.dma_start(lnp[:, 0], ln2_g[bass.ds(l, 1)].to_broadcast([P, D])).then_inc(ln_in.sem, 16)
                sp.dma_start(lnp[:, 1], ln2_b[bass.ds(l, 1)].to_broadcast([P, D])).then_inc(ln_in.sem, 16)
                sp.wait_ge(sh_done.sem, sh_done(l, 1))
                up_load(1, 2)
                wait_alone(sp, rounds_ready, l, 1)
                rounds = sp.value_load(rounds_i[0:1, 0:1], min_val=1, max_val=MAX_ROUNDS)
                with sp.Fori(1, rounds * NQ) as n:
                    q = q_first + n
                    e = (n % NQ) * QUAD
                    sp.wait_ge(up_done[0], q + 1)
                    up_load(0, e)
                    sp.wait_ge(up_done[1], q + 1)
                    up_load(1, e + 2)
                    sp.wait_ge(y_ps, 4 * q)
                    down_load(0, e)
                    down_load(1, e + 2)
                sp.reg_add(quads, quads, rounds * NQ)
            sp.wait_ge(ln.sem, ln(DEPTH, 0))
            sp.dma_start(out.rearrange("b (t p) d -> p (b t) d", p=P), x_tok[:]).then_inc(out_sem, 16)
            sp.wait_ge(out_sem, 16)

        @block.tensor
        def _(pe):
            def split3(o, a_hi, a_lo, b_hi, b_lo, start, stop):
                nc.tensor.matmul(o, a_lo, b_hi, start=start, stop=False, skip_group_check=True)
                nc.tensor.matmul(o, a_hi, b_lo, start=False, stop=False, skip_group_check=True)
                return nc.tensor.matmul(o, a_hi, b_hi, start=False, stop=stop, skip_group_check=True)

            def wait_piece(l, a, n=0, i=0):
                which = (lo_even, lo_odd)[a % 2]
                pe.wait_ge(which.sem, which(l, a // 2 + 1 + (n // 2) * i))

            def chunk_rows(l, c, nc_, a, n, i, b_hi, b_lo, to, first, last):
                s = a % RING
                wait_piece(l, a, n, i)
                for m in range(2):
                    for k in range(PB):
                        mm = split3(to[:, m * S:(m + 1) * S], whi[:, s, k, m * P:(m + 1) * P], wlo[:, s, k, m * P:(m + 1) * P],
                                    b_hi[:, k], b_lo[:, k], first and m == 0 and k == 0, last and k == PB - 1)
                mm.then_inc(used.sem, 1)

            def wide(l, c, a, n=0, i=0, cn=0):
                pe.wait_ge(evac.sem, evac(l, c - 1 + cn * i))
                for half in range(2):
                    chunk_rows(l, c, cn, a + half, n, i, xs_hi[:, half * PB:(half + 1) * PB],
                               xs_lo[:, half * PB:(half + 1) * PB], bank[c % 2], half == 0, half == 1)

            def tall(l, c, a, lhs_hi, lhs_lo):
                pe.wait_ge(evac.sem, evac(l, c - 1))
                for half in range(2):
                    s = (a + half) % RING
                    wait_piece(l, a + half)
                    for t in range(T):
                        for k in range(PB):
                            kk = half * PB + k
                            mm = split3(bank[c % 2][:, t * CW:(t + 1) * CW], lhs_hi[:, kk, t * P:(t + 1) * P],
                                        lhs_lo[:, kk, t * P:(t + 1) * P], whi[:, s, k], wlo[:, s, k],
                                        half == 0 and t == 0 and k == 0, half == 1 and k == PB - 1)
                    mm.then_inc(used.sem, 1)

            def turn_x(done):
                for kk in range(4):
                    for k in range(2):
                        for t in range(T):
                            mm = nc.tensor.transpose(bank[4 + kk][:, k * S + t * P:k * S + (t + 1) * P],
                                                     x_tok[:, t].rearrange("p (q k) -> p k q", k=KD)[:, 2 * kk + k], ident)
                    mm.then_inc(done.sem, 1)

            pe.sem_inc(used.sem, used.credit)
            pe.sem_inc(logit_ps.sem, logit_ps.credit)
            for free in (up_done[0], up_done[1], pick_t_ps):
                pe.sem_inc(free, 1)
            pe.wait_ge(start_in, 18 * 16)
            nc.tensor.transpose(bank[0][:, 0:DEPTH * PAR_ROWS], rows[0:DEPTH * PAR_ROWS, :], ident[0:DEPTH * PAR_ROWS, 0:DEPTH * PAR_ROWS]).then_inc(rows_ps, 1)

            quads = pe.alloc_register("quads_before")
            pe.reg_mov(quads, 0)
            with pe.Fori(0, DEPTH) as l:
                pe.wait_ge(ln.sem, ln(l, 0))
                turn_x(xt_ps)
                pe.wait_ge(start_dve, 3)
                wait_alone(pe, xs_lo_done, l, 4)
                with pe.Fori(0, 2) as i:
                    for u in range(2):
                        wide(l, u, 2 * u, 4, i, 2)
                for u in range(2):
                    wide(l, 4 + u, 8 + 2 * u)
                with pe.Fori(0, 2) as i:
                    for u in range(2):
                        wide(l, C_QK + u, P_QK + 2 * u, 4, i, 2)
                pe.wait_ge(small_in.sem, small_in(l, 48))
                pe.wait_ge(conv_done.sem, conv_done(l, 16))
                for j in range(2):
                    for h in range(H):
                        mm = nc.tensor.matmul(bank[4 + 2 * j + h // 2][:, (h % 2) * S:(h % 2 + 1) * S], small_w[:, 1 + j, h],
                                              conv[:, h], start=True, stop=True)
                    mm.then_inc(ri_ps.sem, 1)
                tall(l, C_V, P_V, xs_hi, xs_lo)
                pe.wait_ge(pool_sum.sem, pool_sum(l, 13))
                for h in range(H):
                    mm = nc.tensor.matmul(bank[2 + h // 2][:, (h % 2) * S:(h % 2 + 1) * S], small_w[:, 0, h], pooled[:, h],
                                          start=True, stop=True)
                mm.then_inc(pl_ps.sem, 1)
                tall(l, C_V + 1, P_V + 2, xs_hi, xs_lo)

                def scores(h):
                    q, k = qk[:, h // 2, (h % 2) * S:(h % 2 + 1) * S], qk[:, 2 + h // 2, (h % 2) * S:(h % 2 + 1) * S]
                    nc.tensor.matmul(bank[4 + h % 2][:, 0:S], k[:, 0:P], q, start=True, stop=True)
                    nc.tensor.matmul(bank[4 + h % 2][:, S:S + P], k[:, P:S], q[:, P:S], start=True, stop=True).then_inc(sc_ps.sem, 1)

                def mix_values(h):
                    v, to = val[:, :, h * P:(h + 1) * P], bank[6 + h // 2][:, (h % 2) * S:(h % 2 + 1) * S]
                    nc.tensor.matmul(to, v[:, 0], decayed[:, h % 2, 0:S], start=h % 2 == 0, stop=False, skip_group_check=True)
                    return nc.tensor.matmul(to[:, P:S], v[:, 1], decayed[:, h % 2, S:S + P], start=False, stop=True, skip_group_check=True)

                pe.wait_ge(roped.sem, roped(l, 4))
                pe.wait_ge(i_done.sem, i_done(l, 4))
                scores(0)
                scores(1)
                wide(l, C_G, P_G)
                pe.wait_ge(evac.sem, evac(l, C_V + 2))
                pe.wait_ge(decayed_done.sem, decayed_done(l, 2))
                mix_values(0)
                mix_values(1).then_inc(o_ps.sem, 1)
                scores(2)
                scores(3)
                wide(l, C_G + 1, P_G + 2)
                pe.wait_ge(decayed_done.sem, decayed_done(l, 4))
                mix_values(2)
                mix_values(3).then_inc(o_ps.sem, 1)
                for pair in range(2):
                    pe.wait_ge(o_sb.sem, o_sb(l, pair + 1))
                    nc.tensor.matmul(bank[4 + pair][:, :], tb("mean"), ret[:, pair], start=True, stop=True).then_inc(mean_ps.sem, 1)

                def gates_chunk(j, v, b_hi, b_lo, i):
                    c = C_GL + v
                    pe.wait_ge(evac.sem, evac(l, c - 1 + 4 * i))
                    a = P_GL + 3 * v
                    for half in range(2):
                        chunk_rows(l, c, 4, a + half, 12, i, xs_hi[:, half * PB:(half + 1) * PB],
                                   xs_lo[:, half * PB:(half + 1) * PB], bank[c % 2], half == 0, half == 1)
                    chunk_rows(l, c, 4, a + 2, 12, i, b_hi, b_lo, bank[2 + c % 2], True, True)

                pe.wait_ge(br_ready.sem, br_ready(l, 4))
                for v in range(4):
                    gates_chunk(0, v, br_hi[:, 0], br_lo[:, 0], 0)
                    if v < 2:
                        pe.wait_ge(o_sq.sem, o_sq(l, v + 1))
                        nc.tensor.matmul(bank[6 + v][:, :], tb("mean"), (tmp1, tmp2)[v][:], start=True, stop=True).then_inc(var_ps.sem, 1)
                with pe.Fori(1, 3) as j:
                    pe.wait_ge(br_ready.sem, br_ready(l, 4 + j))
                    for v in range(4):
                        gates_chunk(j, v, br_hi[:, j % 2], br_lo[:, j % 2], j)
                pe.wait_ge(m_lo_done.sem, m_lo_done(l, 4))
                for o in range(4):
                    tall(l, C_OUT + o, P_OUT + 2 * o, br_hi[:].rearrange("p a k s -> p (a k) s"), br_lo[:].rearrange("p a k s -> p (a k) s"))

                pe.wait_ge(ln.sem, ln(l, 13))
                turn_x(xt2_ps)
                pe.wait_ge(xt2_dve.sem, xt2_dve(l, 2))
                pe.wait_ge(xt2_act.sem, xt2_act(l, 2))
                pe.wait_ge(rw_in.sem, rw_in(l, 16))
                for k in range(KD):
                    mm = nc.tensor.matmul(bank[4][0:N_E, 0:S], rw[:, k], xt[:, k], start=k == 0, stop=k == KD - 1)
                mm.then_inc(logit_ps.sem, 1)
                pe.wait_ge(sh_in.sem, sh_in(l, 48))
                for m in range(2):
                    for j in range(2):
                        for k in range(KD):
                            mm = nc.tensor.matmul(bank[6 + m][:, j * S:(j + 1) * S], shw[:, m, k, j * P:(j + 1) * P], xt[:, k],
                                                  start=k == 0, stop=k == KD - 1)
                    mm.then_inc(sh_ps.sem, 1)
                    if m == 0:
                        pe.wait_ge(biased_t.sem, biased_t(l, 1))
                        for t in range(T):
                            mm = nc.tensor.transpose(bank[5][:, t * P:(t + 1) * P], sc_t[:, t * P:(t + 1) * P], ident)
                        mm.then_inc(sc_tok_ps.sem, 1)
                pe.wait_ge(route.sem, route(l, 32))
                nc.tensor.matmul(bank[4][:, 0:N_E], tb("before"), chosen[:, 0], start=True, stop=True)
                nc.tensor.matmul(bank[4][:, N_E:2 * N_E], tb("before"), chosen[:, 1], start=True, stop=False)
                nc.tensor.matmul(bank[4][:, N_E:2 * N_E], ones, chosen[:, 0], start=False, stop=True)
                nc.tensor.matmul(bank[4][:, 2 * N_E:3 * N_E], ones, chosen[:, 0], start=True, stop=False)
                nc.tensor.matmul(bank[4][:, 2 * N_E:3 * N_E], ones, chosen[:, 1], start=False, stop=True).then_inc(rank_ps.sem, 1)
                pe.wait_ge(sh_h.sem, sh_h(l, 2))
                for t in range(T):
                    for half in range(2):
                        for j in range(2):
                            mm = nc.tensor.matmul(bank[2 * t + half][:, :], m_h_shared[:, j, t * P:(t + 1) * P],
                                                  shw2[:, j, half * 512:(half + 1) * 512], start=j == 0, stop=False, skip_group_check=True)
                mm.then_inc(sh_done.sem, 1)
                wait_alone(pe, rounds_ready, l, 1)
                rounds = pe.value_load(rounds_i[0:1, 0:1], min_val=1, max_val=MAX_ROUNDS)
                q_first = pe.snap(quads)
                wait_alone(pe, tok_lo, l, 2)
                with pe.Fori(0, rounds * NQ) as n:
                    q = q_first + n
                    pe.wait_ge(picked, q + l + 1)
                    for g in range(4):
                        if g == 2:
                            pe.wait_ge(xg_dve, 2 * q + 1)
                        if g == 3:
                            pe.wait_ge(xg_act, 2 * q + 1)
                        for k in range(2):
                            o = bank[4 + g % 2][:, k * S:(k + 1) * S]
                            for t in range(T):
                                for part, x_part in enumerate((xs_lo, xs_hi)):
                                    lhs = x_part[:].rearrange("p k s -> p (k s)")[:, t * D + (2 * g + k) * P:t * D + (2 * g + k + 1) * P]
                                    mm = nc.tensor.matmul(o, lhs, pick[:, t].rearrange("p e c -> p (e c)"),
                                                          start=t == 0 and part == 0, stop=t == 1 and part == 1)
                        mm.then_inc(gathered, 1)
                    pe.wait_ge(xg_dve, 2 * q + 2)
                    pe.wait_ge(xg_act, 2 * q + 2)

                    def up(X):
                        pe.wait_ge(w13_in[X], 32 * q + 32)
                        for k in range(KD):
                            for e in range(2):
                                mm = nc.tensor.matmul(bank[6 + X][64 * e:64 * e + 64, :], xg[:, k, (2 * X + e) * CAP:(2 * X + e + 1) * CAP],
                                                      w13[X][:, :, e, k * FE:(k + 1) * FE], start=k == 0, stop=k == KD - 1,
                                                      skip_group_check=True)
                        mm.then_inc(up_done[X], 1)

                    def turn_h(X):
                        pe.wait_ge(h_done, 2 * q + X + 1)
                        for j in range(2):
                            mm = nc.tensor.transpose(bank[5][:, X * 2 * P + j * P:X * 2 * P + (j + 1) * P], m_h[:, X, j], ident)
                        mm.then_inc(ht_ps, 1)

                    def down(X, half):
                        for j in range(2):
                            for e in range(2):
                                mm = nc.tensor.matmul(bank[6 + half][64 * e:64 * e + 64, :], m_ht[:, X, j, 64 * e:64 * e + 64],
                                                      w2[X][:, e, j * D + half * 512:j * D + (half + 1) * 512],
                                                      start=j == 0, stop=j == 1, skip_group_check=True)
                        mm.then_inc(y_ps, 1)

                    def add(X, half):
                        pe.wait_ge(y_lo_done, 4 * q + 2 * X + half + 1)
                        for t in range(T):
                            for y in (y_lo, y_hi):
                                mm = nc.tensor.matmul(bank[2 * t + half][:, :], pick_t[:, X, t * P:(t + 1) * P], y[:, half],
                                                      start=False, stop=False, skip_group_check=True)
                        return mm

                    up(0)
                    pe.wait_ge(picked_w, q + 1)
                    for X in range(2):
                        for t in range(T):
                            mm = nc.tensor.transpose(bank[4][:, X * S + t * P:X * S + (t + 1) * P],
                                                     pick_w[:, t, 2 * X:2 * X + 2].rearrange("p e c -> p (e c)"), ident)
                    mm.then_inc(pick_t_ps, 1)
                    up(1)
                    turn_h(0)
                    pe.wait_ge(w2_in[0], 16 * q + 16)
                    pe.wait_ge(ht_done, 2 * q + 1)
                    down(0, 0)
                    turn_h(1)
                    down(0, 1)
                    pe.wait_ge(pick_t_done, 2 * q + 2)
                    add(0, 0)
                    add(0, 1)
                    pe.wait_ge(w2_in[1], 16 * q + 16)
                    pe.wait_ge(ht_done, 2 * q + 2)
                    down(1, 0)
                    down(1, 1)
                    add(1, 0)
                    add(1, 1).then_inc(added, 1)
                pe.reg_add(quads, quads, rounds * NQ)

        @block.scalar
        def _(act):
            def copy_hi(o, i):
                return nc.scalar.activation(o, i, ACT.Copy)

            def hi_part(l, a, n=0, i=0):
                s = a % RING
                act.wait_ge(raw_in[s].sem, raw_in[s](l, 16 * (a // RING + 1) + 4 * n * i))
                act.wait_ge(used.sem, used(l, a + 1 - RING + n * i))
                copy_hi(whi[:, s], raw[:, s]).then_inc(hi_done.sem, 1)

            act.wait_ge(start_dve, 4)
            nc.scalar.activation(lam_t[:, 1], lam_t[:, 0], ACT.Exp).then_inc(start_act, 1)
            act.wait_ge(start_dve, 5)
            nc.scalar.activation(rope_c[:], turns[:, 0], ACT.Sin).then_inc(start_act, 1)
            nc.scalar.activation(rope_s[:], turns[:, 1], ACT.Sin).then_inc(start_act, 1)

            quads = act.alloc_register("quads_before")
            act.reg_mov(quads, 0)
            with act.Fori(0, DEPTH) as l:
                hi_part(l, 0)
                hi_part(l, 1)
                for kk in range(4):
                    act.wait_ge(xt_ps.sem, xt_ps(l, kk + 1))
                    copy_hi(xs_hi[:, 2 * kk:2 * kk + 2].rearrange("p k s -> p (k s)"), bank[4 + kk][:, :]).then_inc(xs_hi_done.sem, 1)
                with act.Fori(0, 2) as i:
                    for u in range(2, 6):
                        hi_part(l, u, 4, i)
                for a in range(10, 14):
                    hi_part(l, a)
                with act.Fori(0, 2) as i:
                    for u in range(4):
                        hi_part(l, P_QK + 2 + u, 4, i)
                act.wait_ge(par_ready.sem, par_ready(l, 2))
                act.wait_ge(ri_ps.sem, ri_ps(l, 1))
                for h in range(H):
                    nc.scalar.activation(rg[:, h], bank[4 + h // 2][:, (h % 2) * S:(h % 2 + 1) * S], ACT.Sigmoid,
                                         bias=parl[:, BA + h:BA + h + 1]).then_inc(r_done.sem, 1)
                act.wait_ge(ri_ps.sem, ri_ps(l, 2))
                for h in range(H):
                    nc.scalar.activation(ig[:, h], bank[6 + h // 2][:, (h % 2) * S:(h % 2 + 1) * S], ACT.Sigmoid,
                                         bias=parl[:, BX + h:BX + h + 1]).then_inc(i_done.sem, 1)
                hi_part(l, P_V + 2)
                hi_part(l, P_V + 3)
                act.wait_ge(conv_done.sem, conv_done(l, 16))
                act.wait_ge(evac.sem, evac(l, 6))
                nc.scalar.activation(gelu[:], yr, ACT.Square).then_inc(gelu_sq.sem, 1)
                act.wait_ge(r_done.sem, r_done(l, 4))
                for h in range(H):
                    nc.scalar.activation(ag[:, h], rg[:, h], ACT.Exp, scale=parl[:, NSP8 + h:NSP8 + h + 1]).then_inc(a_done.sem, 1)
                act.wait_ge(a_done.sem, a_done(l, 4))
                for h in range(H):
                    nc.scalar.activation(rg[:, h], rg[:, h], ACT.Tanh, scale=parl[:, SP8 + h:SP8 + h + 1]).then_inc(u_done.sem, 1)
                hi_part(l, P_G)
                hi_part(l, P_G + 1)
                act.wait_ge(pl_ps.sem, pl_ps(l, 1))
                for h in range(H):
                    nc.scalar.activation(br_hi[:, 0, h], bank[2 + h // 2][:, (h % 2) * S:(h % 2 + 1) * S], ACT.Copy,
                                         scale=parl[:, PSC + h:PSC + h + 1]).then_inc(br_hi_done.sem, 1)
                hi_part(l, P_G + 2)
                hi_part(l, P_G + 3)
                act.wait_ge(gelu_cube.sem, gelu_cube(l, 1))
                nc.scalar.activation(gelu[:], gelu[:], ACT.Tanh, scale=0.7978845608028654).then_inc(gelu_tanh.sem, 1)
                act.wait_ge(used.sem, used(l, P_G + 2))
                nc.scalar.activation(sg[:], bank[0][:, :], ACT.Sigmoid).then_inc(g_sg.sem, 1)
                act.wait_ge(o_ps.sem, o_ps(l, 1))
                nc.scalar.activation(ret[:, 0], bank[6][:, :], ACT.Copy).then_inc(o_sb.sem, 1)
                for a in range(3):
                    hi_part(l, P_GL + a)
                act.wait_ge(used.sem, used(l, P_G + 4))
                act.wait_ge(evac.sem, evac(l, C_G + 1))
                nc.scalar.activation(sg[:], bank[1][:, :], ACT.Sigmoid).then_inc(g_sg.sem, 1)
                act.wait_ge(o_ps.sem, o_ps(l, 2))
                nc.scalar.activation(ret[:, 1], bank[7][:, :], ACT.Copy).then_inc(o_sb.sem, 1)
                act.wait_ge(lru.sem, lru(l, 4))
                nc.scalar.activation(rg[:], rg[:], ACT.Sqrt, scale=2.0).then_inc(lru_root.sem, 1)
                for pair in range(2):
                    act.wait_ge(o_dev.sem, o_dev(l, pair + 1))
                    nc.scalar.activation((tmp1, tmp2)[pair][:], ret[:, pair], ACT.Square).then_inc(o_sq.sem, 1)

                def gates(j, v, b, i, first):
                    for a in range(3):
                        hi_part(l, P_GL + 3 * (v + 1) + a, 12, i)
                    act.wait_ge(used.sem, used(l, P_GL + 3 * v + 2 + 12 * i))
                    if first and v == 0:
                        act.wait_ge(evac.sem, evac(l, C_GL))
                    else:
                        act.wait_ge(merge_done.sem, merge_done(l, v + 4 * i))
                    for m in range(2):
                        nc.scalar.activation(sg[:, m * S:(m + 1) * S], bank[v % 2][:, m * S:(m + 1) * S], ACT.Sigmoid,
                                             bias=parl[:, bass.ds(b * KD + (GB + 2 * v + m), 1)]).then_inc(gates_sg.sem, 1)

                for v in range(4):
                    gates(0, v, 1, 0, True)
                    if v == 1:
                        act.wait_ge(lru.sem, lru(l, 10))
                        copy_hi(br_hi[:, 1], rg[:]).then_inc(br_hi_done.sem, 1)
                    if v == 2:
                        for pair in range(2):
                            act.wait_ge(var_ps.sem, var_ps(l, pair + 1))
                            nc.scalar.activation((tmp1, tmp2)[pair][:], bank[6 + pair][:, :], ACT.Sqrt, bias=eps[:, 1:2]).then_inc(o_sd.sem, 1)
                act.wait_ge(o_norm.sem, o_norm(l, 6))
                act.wait_ge(used.sem, used(l, P_GL + 12))
                copy_hi(br_hi[:, 0], ret[:].rearrange("p a (k s) -> p (a k) s", s=S)).then_inc(br_hi_done.sem, 1)
                with act.Fori(1, 3) as j:
                    for v in range(4):
                        gates(j, v, (j + 1) % 3, j, False)
                for o in range(4):
                    act.wait_ge(merge_done.sem, merge_done(l, 8 + o + 1))
                    act.wait_ge(used.sem, used(l, P_OUT))
                    copy_hi(br_hi[:].rearrange("p a k s -> p (a k s)")[:, 2 * o * S:2 * (o + 1) * S], merged[:, o]).then_inc(m_hi_done.sem, 1)
                for a in range(3, 8):
                    hi_part(l, P_OUT + a)
                act.wait_ge(ln.sem, ln(l, 6))
                nc.scalar.activation(sd[:], mv[:, :, 1], ACT.Sqrt, bias=eps[:, 0:1]).then_inc(ln_sd.sem, 1)
                act.wait_ge(ln.sem, ln(l, 13))
                for kk in (1, 3):
                    act.wait_ge(xt2_ps.sem, xt2_ps(l, kk + 1))
                    nc.scalar.activation(xt[:, 2 * kk:2 * kk + 2].rearrange("p k s -> p (k s)"), bank[4 + kk][:, :], ACT.Copy).then_inc(xt2_act.sem, 1)
                act.wait_ge(logit_ps.sem, logit_ps(l, 1))
                nc.scalar.activation(sc_t[0:N_E, :], bank[4][0:N_E, 0:S], ACT.Sigmoid).then_inc(sig_t.sem, 1)
                for t in range(T):
                    copy_hi(xs_hi[:].rearrange("p k s -> p (k s)")[:, t * D:(t + 1) * D].rearrange("p (k q) -> p k q", k=KD),
                            x_tok[:, t].rearrange("p (q k) -> p k q", k=KD)).then_inc(tok_hi.sem, 1)
                act.wait_ge(sh_ps.sem, sh_ps(l, 1))
                nc.scalar.activation(shared_sg, bank[6][:, :], ACT.Sigmoid).then_inc(sh_sg.sem, 1)
                wait_alone(act, rounds_ready, l, 1)
                rounds = act.value_load(rounds_i[0:1, 0:1], min_val=1, max_val=MAX_ROUNDS)
                q_first = act.snap(quads)
                with act.Fori(0, rounds * NQ) as n:
                    q = q_first + n
                    for g in (1, 3):
                        act.wait_ge(gathered, 4 * q + g + 1)
                        nc.scalar.activation(xg[:, 2 * g:2 * g + 2].rearrange("p k s -> p (k s)"), bank[5][:, :], ACT.Copy).then_inc(xg_act, 1)

                    def act_h(X):
                        act.wait_ge(up_done[X], q + 2)
                        nc.scalar.activation(m_sg[:, X], bank[6 + X][:, 0:FE], ACT.Sigmoid).then_inc(h_sg, 1)

                    def ht_out(X):
                        act.wait_ge(ht_ps, 2 * q + X + 1)
                        nc.scalar.activation(m_ht[:, X].rearrange("p j s -> p (j s)"), bank[5][:, X * 2 * P:(X + 1) * 2 * P], ACT.Copy).then_inc(ht_done, 1)

                    def y_out(X, half):
                        act.wait_ge(y_ps, 4 * q + 2 * X + half + 1)
                        nc.scalar.activation(y_hi[:, half], bank[6 + half][:, :], ACT.Copy, scale=slot_gate[:, X:X + 1]).then_inc(y_hi_done, 1)

                    act_h(0)
                    act_h(1)
                    ht_out(0)
                    act.wait_ge(pick_t_done, 2 * q + 2)
                    y_out(0, 0)
                    ht_out(1)
                    y_out(0, 1)
                    y_out(1, 0)
                    y_out(1, 1)
                act.reg_add(quads, quads, rounds * NQ)
                act.wait_ge(ln.sem, ln(l, 19))
                nc.scalar.activation(sd[:], mv[:, :, 1], ACT.Sqrt, bias=eps[:, 0:1]).then_inc(ln_sd.sem, 1)

        @block.gpsimd
        def _(pool):
            g = nc.gpsimd
            pool.sem_inc(lo_even.sem, lo_even.credit)
            quads = pool.alloc_register("quads_before")
            pool.reg_mov(quads, 0)
            with pool.Fori(0, DEPTH) as l:
                lo_part(pool, g, l, 0)
                with pool.Fori(0, 2) as i:
                    for u in (2, 4):
                        lo_part(pool, g, l, u, 4, i)
                count = [0]

                def step(ins):
                    count[0] += 1
                    ins.then_inc(pool_sum.sem, 1)
                    wait_alone(pool, pool_sum, l, count[0])

                pool.wait_ge(evac.sem, evac(l, 2))
                step(g.tensor_tensor(pooled[:, :, 1:], xp[:, :, 1:], xp[:, :, :-1], ALU.add))
                lo_part(pool, g, l, 10)
                step(g.tensor_copy(pooled[:, :, 0:1], xp[:, :, 0:1]))
                step(g.tensor_tensor(pool_b[:, 1:, 2:], pooled[:, 1:, 2:], pooled[:, 1:, :-2], ALU.add))
                step(g.tensor_copy(pool_b[:, 1:, 0:2], pooled[:, 1:, 0:2]))
                lo_part(pool, g, l, 12)
                step(g.tensor_tensor(pooled[:, 2:, 4:], pool_b[:, 2:, 4:], pool_b[:, 2:, :-4], ALU.add))
                step(g.tensor_copy(pooled[:, 2:, 0:4], pool_b[:, 2:, 0:4]))
                step(g.tensor_tensor(pool_b[:, 3:, 8:], pooled[:, 3:, 8:], pooled[:, 3:, :-8], ALU.add))
                step(g.tensor_copy(pool_b[:, 3:, 0:8], pooled[:, 3:, 0:8]))
                inv_n = tb("inv_n").rearrange("p (h s) -> p h s", h=H)
                with pool.Fori(0, 2) as i:
                    for u in (2, 4):
                        lo_part(pool, g, l, P_QK + u, 4, i)
                for h in range(H):
                    src = (pooled, pool_b)[h % 2]
                    step(g.tensor_tensor(pooled[:, h], src[:, h], inv_n[:, h], ALU.mult))
                step(g.tensor_tensor(pooled[:], pooled[:], xp, ALU.subtract))
                lo_part(pool, g, l, P_V + 2)
                lo_part(pool, g, l, P_G)
                pool.wait_ge(gelu_arg.sem, gelu_arg(l, 1))
                g.tensor_tensor(gelu[:], gelu[:], yr, ALU.mult).then_inc(gelu_cube.sem, 1)
                lo_part(pool, g, l, P_G + 2)
                lo_part(pool, g, l, P_GL)
                lo_part(pool, g, l, P_GL + 2)
                for a in range(4, 16, 2):
                    lo_part(pool, g, l, P_GL + a)
                with pool.Fori(1, 3) as j:
                    for a in range(4, 16, 2):
                        lo_part(pool, g, l, P_GL + a, 12, j)
                for a in (4, 6):
                    lo_part(pool, g, l, P_OUT + a)
                for t in range(T):
                    pool.wait_ge(tok_hi.sem, tok_hi(l, t + 1))
                    g.tensor_tensor(xs_lo[:].rearrange("p k s -> p (k s)")[:, t * D:(t + 1) * D].rearrange("p (k q) -> p k q", k=KD),
                                    x_tok[:, t].rearrange("p (q k) -> p k q", k=KD),
                                    xs_hi[:].rearrange("p k s -> p (k s)")[:, t * D:(t + 1) * D].rearrange("p (k q) -> p k q", k=KD).bitcast(F32),
                                    ALU.subtract).then_inc(tok_lo.sem, 1)
                wait_alone(pool, rounds_ready, l, 1)
                rounds = pool.value_load(rounds_i[0:1, 0:1], min_val=1, max_val=MAX_ROUNDS)
                q_first = pool.snap(quads)
                with pool.Fori(0, rounds * NQ) as n:
                    q = q_first + n
                    pool.wait_ge(picked, q + l + 1)
                    pool.wait_ge(pick_t_ps, q + 1)
                    gate = weight[:].rearrange("p t (q e) -> p t q e", e=QUAD)
                    for t in range(T):
                        ins = g.tensor_tensor(pick_w[:, t], pick[:, t].bitcast(F32),
                                              gate[:, t, n % NQ].unsqueeze(2).to_broadcast([P, QUAD, CAP]), ALU.mult)
                    ins.then_inc(picked_w, 1)
                pool.reg_add(quads, quads, rounds * NQ)

        @block.vector
        def _(dve):
            v_ = nc.vector

            def seq(signal, l, first=0):
                count = [first]

                def step(ins):
                    count[0] += 1
                    ins.then_inc(signal.sem, 1)
                    dve.wait_ge(signal.sem, signal(l, count[0]))
                return step

            for free in (evac, lo_odd, roped, ln):
                dve.sem_inc(free.sem, free.credit)
            v_.memset(eps[:, 0:1], LN_EPS).then_inc(start_dve, 1)
            v_.memset(eps[:, 1:2], GN_EPS).then_inc(start_dve, 1)
            dve.wait_ge(rows_ps, 1)
            v_.tensor_copy(par[:, :, 0:PAR_ROWS], bank[0][:, 0:DEPTH * PAR_ROWS].rearrange("p (l r) -> p l r", l=DEPTH)).then_inc(start_dve, 1)
            dve.wait_ge(start_dve, 3)
            v_.scalar_tensor_tensor(lam_t[:, 0], par[:, :, LAM:LAM + H], -1.0, par[:, :, LAM:LAM + H], ALU.mult, ALU.min).then_inc(start_dve, 1)
            dve.wait_ge(start_in, 18 * 16)
            step = seq(start_chain, 0)
            step(v_.tensor_copy(ang[:], pos_i[:]))
            step(v_.tensor_scalar(ang[:], ang[:], tb("freq"), None, ALU.mult))
            two_pi, magic = 2 * np.pi, 1.5 * 2.0 ** 23
            c1 = 6.28125
            c2 = float(np.float32(np.round((two_pi - c1) * 2 ** 21) / 2 ** 21))
            c3 = two_pi - c1 - c2
            step(v_.tensor_scalar(turns[:, 0], ang[:], 1.0 / two_pi, 0.25, ALU.mult, ALU.add))
            step(v_.tensor_scalar(turns[:, 1], ang[:], 1.0 / two_pi, None, ALU.mult))
            step(v_.tensor_scalar(turns[:], turns[:], magic, None, ALU.add))
            step(v_.tensor_scalar(turns[:], turns[:], magic, None, ALU.subtract))
            ang2 = ang[:].unsqueeze(1).to_broadcast([P, 2, S])
            step(v_.scalar_tensor_tensor(reduced[:], turns[:], -c1, ang2, ALU.mult, ALU.add))
            step(v_.scalar_tensor_tensor(reduced[:], turns[:], -c2, reduced[:], ALU.mult, ALU.add))
            step(v_.scalar_tensor_tensor(reduced[:], turns[:], -c3, reduced[:], ALU.mult, ALU.add))
            step(v_.tensor_scalar(reduced[:, 0], reduced[:, 0], np.pi / 2, None, ALU.add))
            pi = float(np.nextafter(np.float32(np.pi), np.float32(0)))
            v_.tensor_scalar(turns[:], reduced[:], pi, -pi, ALU.min, ALU.max).then_inc(start_dve, 1)
            dve.wait_ge(start_act, 1)
            step(v_.tensor_scalar(lam_t[:, 2], lam_t[:, 1], 2.0, None, ALU.add))
            step(v_.reciprocal(lam_t[:, 2], lam_t[:, 2]))
            step(v_.tensor_tensor(lam_t[:, 1], lam_t[:, 1], lam_t[:, 2], ALU.mult))
            step(v_.tensor_tensor(lam_t[:, 2], lam_t[:, 1], lam_t[:, 1], ALU.mult))
            step(v_.tensor_scalar(lam_t[:, 3], lam_t[:, 2], 1.0 / 17, None, ALU.mult))
            for c in (15, 13, 11, 9, 7, 5, 3):
                step(v_.scalar_tensor_tensor(lam_t[:, 3], lam_t[:, 3], 1.0 / c, lam_t[:, 2], ALU.add, ALU.mult))
            step(v_.scalar_tensor_tensor(lam_t[:, 3], lam_t[:, 3], 1.0, lam_t[:, 1], ALU.add, ALU.mult))
            step(v_.tensor_scalar(lam_t[:, 2], par[:, :, LAM:LAM + H], -1.0, 0.0, ALU.mult, ALU.max))
            step(v_.scalar_tensor_tensor(lam_t[:, 2], lam_t[:, 3], 2.0, lam_t[:, 2], ALU.mult, ALU.add))
            step(v_.tensor_scalar(par[:, :, SP8:SP8 + H], lam_t[:, 2], RG_C, None, ALU.mult))
            step(v_.tensor_scalar(par[:, :, NSP8:NSP8 + H], lam_t[:, 2], -RG_C, None, ALU.mult))
            dve.wait_ge(start_act, 3)
            step(v_.tensor_scalar(rope_s[:], rope_s[:], tb("sign"), None, ALU.mult))

            def lo(l, a, n=0, i=0):
                lo_part(dve, v_, l, a, n, i)

            def norm(l, call, z_wait):
                base = 13 * call
                for t in range(T):
                    for half in range(2):
                        v_.bn_stats(stats[:, t, half], x_tok[:, t, half * 512:(half + 1) * 512]).then_inc(ln.sem, 1)
                wait_alone(dve, ln, l, base + 4)
                for t in range(T):
                    v_.bn_aggr(mv[:, t], stats[:, t].rearrange("p a b -> p (a b)")).then_inc(ln.sem, 1)
                dve.wait_ge(ln_sd.sem, ln_sd(l, call + 1))
                v_.reciprocal(sd[:], sd[:]).then_inc(ln.sem, 1)
                dve.wait_ge(ln.sem, ln(l, base + 7))
                for t in range(T):
                    v_.tensor_scalar(x_tok[:, t], x_tok[:, t], mv[:, t, 0:1], sd[:, t:t + 1], ALU.subtract, ALU.mult).then_inc(ln.sem, 1)
                dve.wait_ge(ln_in.sem, ln_in(l, 32 * (call + 1)))
                for j, op in enumerate((ALU.mult, ALU.add)):
                    for t in range(T):
                        dve.wait_ge(ln.sem, ln(l, base + 8 + 2 * j + t))
                        v_.tensor_tensor(x_tok[:, t], x_tok[:, t], lnp[:, j], op).then_inc(ln.sem, 1)

            quads = dve.alloc_register("quads_before")
            dve.reg_mov(quads, 0)
            with dve.Fori(0, DEPTH) as l:
                v_.tensor_copy(parl[:], par[:, l]).then_inc(par_ready.sem, 1)
                v_.tensor_copy(rbl[0:N_E, :], rbias[0:N_E, bass.ds(l, 1)]).then_inc(par_ready.sem, 1)
                lo(l, 1)
                for kk in range(4):
                    dve.wait_ge(xs_hi_done.sem, xs_hi_done(l, kk + 1))
                    v_.tensor_tensor(xs_lo[:, 2 * kk:2 * kk + 2].rearrange("p k s -> p (k s)"), bank[4 + kk][:, :],
                                     xs_hi[:, 2 * kk:2 * kk + 2].rearrange("p k s -> p (k s)").bitcast(F32), ALU.subtract).then_inc(xs_lo_done.sem, 1)
                with dve.Fori(0, 2) as i:
                    for u in range(2):
                        lo(l, 2 * u + 3, 4, i)
                        dve.wait_ge(used.sem, used(l, 2 * u + 2 + 4 * i))
                        v_.tensor_copy(mix[:, bass.ds(2 * i + u, 1)].rearrange("p a s -> p (a s)"), bank[u][:, :]).then_inc(evac.sem, 1)
                dve.wait_ge(evac.sem, evac(l, 4))
                dve.wait_ge(par_ready.sem, par_ready(l, 2))

                def conv_tap(k):
                    for h in range(H):
                        w = parl[:, CVW + 4 * k + h:CVW + 4 * k + h + 1]
                        if k == 0:
                            v_.tensor_scalar(conv[:, h], xr[:, h], w, parl[:, CVB + h:CVB + h + 1], ALU.mult, ALU.add).then_inc(conv_done.sem, 1)
                        else:
                            dve.wait_ge(conv_done.sem, conv_done(l, 4 * (k - 1) + h + 1))
                            v_.scalar_tensor_tensor(conv[:, h, k:], xr[:, h, :-k], w, conv[:, h, k:], ALU.mult, ALU.add).then_inc(conv_done.sem, 1)

                for u in range(2):
                    lo(l, 11 + 2 * u)
                    conv_tap(2 * u)
                    dve.wait_ge(used.sem, used(l, 8 + 2 * u + 2))
                    v_.tensor_copy(mix[:, 4 + u], bank[u][:, :]).then_inc(evac.sem, 1)
                    conv_tap(2 * u + 1)
                with dve.Fori(0, 2) as i:
                    for u in range(2):
                        lo(l, P_QK + 2 * u + 3, 4, i)
                        dve.wait_ge(used.sem, used(l, P_QK + 2 * u + 2 + 4 * i))
                        dve.wait_ge(roped.sem, roped(l, u + 2 * i))
                        b3 = bank[u][:, :].rearrange("p (h s) -> p h s", h=2)
                        t1, t2 = tmp1[:].rearrange("p (h s) -> p h s", h=2), tmp2[:].rearrange("p (h s) -> p h s", h=2)
                        v_.tensor_tensor(t1, b3, rope_c[:].unsqueeze(1).to_broadcast([P, 2, S]), ALU.mult).then_inc(rope_m.sem, 1)
                        v_.tensor_tensor(t2[0:64], b3[64:128], rope_s[0:64, :].unsqueeze(1).to_broadcast([64, 2, S]), ALU.mult).then_inc(rope_m.sem, 1)
                        v_.tensor_tensor(t2[64:128], b3[0:64], rope_s[64:128, :].unsqueeze(1).to_broadcast([64, 2, S]), ALU.mult).then_inc(evac.sem, 1)
                        dve.wait_ge(rope_m.sem, rope_m(l, 2 * u + 2 + 4 * i))
                        dve.wait_ge(evac.sem, evac(l, C_QK + u + 1 + 2 * i))
                        v_.tensor_tensor(qk[:, bass.ds(u + 2 * i, 1)].rearrange("p a s -> p (a s)"), tmp1[:], tmp2[:], ALU.add).then_inc(roped.sem, 1)

                def values(c):
                    dve.wait_ge(used.sem, used(l, P_V + 2 * c + 2))
                    v_.tensor_copy(val[:, :, c * CW:(c + 1) * CW], bank[c][:, :].rearrange("p (t c) -> p t c", t=T)).then_inc(evac.sem, 1)

                def decay(h):
                    dve.wait_ge(sc_ps.sem, sc_ps(l, h + 1))
                    if h >= 2:
                        dve.wait_ge(o_ps.sem, o_ps(l, 1))
                    else:
                        dve.wait_ge(pool_sum.sem, pool_sum(l, 13))
                    masks = tb("decay_in")[:, h * P:(h + 1) * P], tb("decay_across")[:, h * P:(h + 1) * P]
                    b3 = bank[4 + h % 2]
                    v_.tensor_tensor(decayed[:, h % 2, P:S], b3[:, P:S], masks[1], ALU.mult)
                    v_.tensor_tensor(decayed[:, h % 2, 0:P], b3[:, 0:P], masks[0], ALU.mult)
                    v_.tensor_tensor(decayed[:, h % 2, S:S + P], b3[:, S:S + P], masks[0], ALU.mult).then_inc(decayed_done.sem, 1)

                lo(l, P_V + 3)
                values(0)
                dve.wait_ge(gelu_sq.sem, gelu_sq(l, 1))
                v_.tensor_scalar(gelu[:], gelu[:], 0.044715, 1.0, ALU.mult, ALU.add).then_inc(gelu_arg.sem, 1)
                chain = seq(lru, l)
                dve.wait_ge(i_done.sem, i_done(l, 4))
                chain(v_.tensor_tensor(ig[:], ig[:], conv[:], ALU.mult))
                lo(l, P_G + 1)
                values(1)
                decay(0)
                decay(1)
                dve.wait_ge(u_done.sem, u_done(l, 4))
                chain(v_.tensor_scalar(recip_u[:], rg[:], 1.0, None, ALU.add))
                chain(v_.reciprocal(recip_u[:], recip_u[:]))
                chain(v_.scalar_tensor_tensor(rg[:], rg[:], 1e-34, recip_u[:], ALU.max, ALU.mult))
                lo(l, P_G + 3)
                for h in range(H):
                    dve.wait_ge(br_hi_done.sem, br_hi_done(l, h + 1))
                    v_.scalar_tensor_tensor(br_lo[:, 0, h], bank[2 + h // 2][:, (h % 2) * S:(h % 2 + 1) * S], parl[:, PSC + h:PSC + h + 1],
                                            br_hi[:, 0, h].bitcast(F32), ALU.mult, ALU.subtract).then_inc(br_ready.sem, 1)
                dve.wait_ge(g_sg.sem, g_sg(l, 1))
                v_.tensor_tensor(gate_g[:, 0], bank[0][:, :], sg[:], ALU.mult).then_inc(evac.sem, 1)
                decay(2)
                decay(3)
                lo(l, P_GL + 1)
                dve.wait_ge(g_sg.sem, g_sg(l, 2))
                v_.tensor_tensor(gate_g[:, 1], bank[1][:, :], sg[:], ALU.mult).then_inc(evac.sem, 1)
                for pair in range(2):
                    dve.wait_ge(mean_ps.sem, mean_ps(l, pair + 1))
                    v_.tensor_tensor(ret[:, pair], ret[:, pair], bank[4 + pair][:, :], ALU.subtract).then_inc(o_dev.sem, 1)
                dve.wait_ge(gelu_tanh.sem, gelu_tanh(l, 1))
                v_.scalar_tensor_tensor(gelu[:], gelu[:], 1.0, yr, ALU.add, ALU.mult).then_inc(gelu_gate.sem, 1)

                def merge(v, i, first):
                    dve.wait_ge(gates_sg.sem, gates_sg(l, 2 * v + 2 + 8 * i))
                    dve.wait_ge(used.sem, used(l, P_GL + 3 * v + 3 + 12 * i))
                    if first:
                        v_.tensor_tensor(merged[:, v], sg[:], bank[2 + v % 2][:, :], ALU.mult).then_inc(evac.sem, 1)
                        dve.wait_ge(evac.sem, evac(l, C_GL + v + 1))
                        dve.sem_inc(merge_done.sem, 1)
                    else:
                        v_.tensor_tensor(sg[:], sg[:], bank[2 + v % 2][:, :], ALU.mult).then_inc(evac.sem, 1)
                        dve.wait_ge(evac.sem, evac(l, C_GL + v + 1 + 4 * i))
                        v_.tensor_tensor(merged[:, v], merged[:, v], sg[:], ALU.add).then_inc(merge_done.sem, 1)

                def lru_scan(h):
                    v_.tensor_tensor_scan(hid[:, h], ag[:, h], ig[:, h], 0.0, ALU.mult, ALU.add).then_inc(lru.sem, 1)

                def unit_norm(pair, k):
                    tmp = (tmp1, tmp2)[pair]
                    if k == 0:
                        dve.wait_ge(o_sd.sem, o_sd(l, pair + 1))
                        v_.reciprocal(tmp[:], tmp[:]).then_inc(o_norm.sem, 1)
                    elif k == 1:
                        dve.wait_ge(o_norm.sem, o_norm(l, pair + 1))
                        v_.tensor_tensor(ret[:, pair], ret[:, pair], tmp[:], ALU.mult).then_inc(o_norm.sem, 1)
                    else:
                        dve.wait_ge(o_norm.sem, o_norm(l, pair + 3))
                        v_.tensor_tensor(ret[:, pair], ret[:, pair], gate_g[:, pair], ALU.mult).then_inc(o_norm.sem, 1)

                lo(l, P_GL + 3)
                lo(l, P_GL + 5)
                dve.wait_ge(lru_root.sem, lru_root(l, 1))
                chain(v_.tensor_tensor(ig[:], rg[:], ig[:], ALU.mult))
                dve.wait_ge(a_done.sem, a_done(l, 4))
                lru_scan(0)
                merge(0, 0, True)
                lo(l, P_GL + 7)
                lru_scan(1)
                lru_scan(2)
                lru_scan(3)
                dve.wait_ge(gelu_gate.sem, gelu_gate(l, 1))
                dve.wait_ge(lru.sem, lru(l, 9))
                v_.scalar_tensor_tensor(rg[:], hid[:], 0.5, gelu[:], ALU.mult, ALU.mult).then_inc(lru.sem, 1)
                merge(1, 0, True)
                lo(l, P_GL + 9)
                lo(l, P_GL + 11)
                dve.wait_ge(br_hi_done.sem, br_hi_done(l, 5))
                v_.tensor_tensor(br_lo[:, 1], rg[:], br_hi[:, 1].bitcast(F32), ALU.subtract).then_inc(br_ready.sem, 1)
                merge(2, 0, True)
                lo(l, P_GL + 13)
                for k in range(3):
                    unit_norm(0, k)
                    unit_norm(1, k)
                merge(3, 0, True)
                dve.wait_ge(br_hi_done.sem, br_hi_done(l, 6))
                v_.tensor_tensor(br_lo[:, 0], ret[:].rearrange("p a (k s) -> p (a k) s", s=S), br_hi[:, 0].bitcast(F32), ALU.subtract).then_inc(br_ready.sem, 1)
                with dve.Fori(1, 3) as j:
                    for v, odd in enumerate(((3, 5), (7,), (9, 11), (13,))):
                        for a in odd:
                            lo(l, P_GL + a, 12, j)
                        merge(v, j, False)
                for o in range(4):
                    dve.wait_ge(m_hi_done.sem, m_hi_done(l, o + 1))
                    v_.tensor_tensor(br_lo[:].rearrange("p a k s -> p (a k s)")[:, 2 * o * S:2 * (o + 1) * S], merged[:, o],
                                     br_hi[:].rearrange("p a k s -> p (a k s)")[:, 2 * o * S:2 * (o + 1) * S].bitcast(F32), ALU.subtract).then_inc(m_lo_done.sem, 1)
                for o in range(4):
                    if o < 3:
                        lo(l, P_OUT + 2 * o + 3)
                    dve.wait_ge(used.sem, used(l, P_OUT + 2 * o + 2))
                    z = x_tok[:, :, o * CW:(o + 1) * CW]
                    v_.scalar_tensor_tensor(z, z, ALPHA, bank[o % 2][:, :].rearrange("p (t c) -> p t c", t=T), ALU.mult, ALU.add).then_inc(evac.sem, 1)
                dve.wait_ge(evac.sem, evac(l, N_CHUNKS))
                norm(l, 0, None)

                for kk in (0, 2):
                    dve.wait_ge(xt2_ps.sem, xt2_ps(l, kk + 1))
                    v_.tensor_copy(xt[:, 2 * kk:2 * kk + 2].rearrange("p k s -> p (k s)"), bank[4 + kk][:, :]).then_inc(xt2_dve.sem, 1)
                dve.wait_ge(sig_t.sem, sig_t(l, 1))
                v_.tensor_scalar(sc_t[N_E:2 * N_E, :], sc_t[0:N_E, :], rbl[0:N_E, 0:1], None, ALU.add).then_inc(biased_t.sem, 1)
                dve.wait_ge(sc_tok_ps.sem, sc_tok_ps(l, 1))
                pick_step = seq(route, l)
                v_.tensor_copy(sc[:].rearrange("p t a e -> p (t a e)"), bank[5][:, 0:T * P]).then_inc(route.sem, 1)
                wait_alone(dve, route, l, 1)
                for t in range(T):
                    for e in range(E_GROUPS):
                        v_.max(g8[:, t, e], sc[:, t, 1, e * 8:(e + 1) * 8]).then_inc(route.sem, 1)
                dve.wait_ge(route.sem, route(l, 17))
                pick_step = seq(route, l, 17)
                pick_step(v_.tensor_tensor(grp[:], g8[:, :, :, 0], g8[:, :, :, 1], ALU.add))
                g_flat = grp[:].rearrange("p t g -> p (t g)")
                g_own = g_flat.unsqueeze(2).to_broadcast([P, T * E_GROUPS, E_GROUPS])
                g_all = grp[:].unsqueeze(2).to_broadcast([P, T, E_GROUPS, E_GROUPS])
                c4 = cmp_a[:].rearrange("p (t i) j -> p t i j", t=T)
                d4 = cmp_b[:].rearrange("p (t i) j -> p t i j", t=T)
                o4 = grp[:].unsqueeze(3).to_broadcast([P, T, E_GROUPS, E_GROUPS])
                v_.tensor_tensor(c4, g_all, o4, ALU.is_gt).then_inc(route.sem, 1)
                v_.tensor_tensor(d4, g_all, o4, ALU.is_equal).then_inc(route.sem, 1)
                dve.wait_ge(route.sem, route(l, 20))
                pick_step = seq(route, l, 20)
                lower = tb("lower").unsqueeze(1).to_broadcast([P, T, E_GROUPS * E_GROUPS])
                pick_step(v_.tensor_tensor(cmp_b[:].rearrange("p (t i) j -> p t (i j)", t=T), cmp_b[:].rearrange("p (t i) j -> p t (i j)", t=T), lower, ALU.mult))
                pick_step(v_.tensor_tensor(cmp_a[:], cmp_a[:], cmp_b[:], ALU.add))
                pick_step(v_.tensor_reduce(gpen[:].rearrange("p t g -> p (t g)"), cmp_a[:], AX.X, ALU.add))
                pick_step(v_.tensor_scalar(gmask[:], gpen[:], float(TOP_GROUPS), None, ALU.is_lt))
                pick_step(v_.tensor_scalar(gpen[:], gmask[:], 1.0, BIG, ALU.subtract, ALU.mult))
                m4 = masked[:].rearrange("p t (g e) -> p t g e", g=E_GROUPS)
                biased4 = sc[:, :, 1].rearrange("p t (g e) -> p t g e", g=E_GROUPS)
                pick_step(v_.tensor_tensor(m4, biased4, gmask[:].unsqueeze(3).to_broadcast([P, T, E_GROUPS, 8]), ALU.mult))
                v_.tensor_tensor(m4, m4, gpen[:].unsqueeze(3).to_broadcast([P, T, E_GROUPS, 8]), ALU.add).then_inc(route.sem, 1)
                wait_alone(dve, route, l, 27)
                for t in range(T):
                    v_.max(best[:, t], masked[:, t]).then_inc(route.sem, 1)
                wait_alone(dve, route, l, 29)
                for t in range(T):
                    v_.match_replace(taken[:, t], best[:, t], masked[:, t], -3 * BIG).then_inc(route.sem, 1)
                dve.wait_ge(route.sem, route(l, 31))
                v_.tensor_tensor(chosen[:], masked[:], taken[:], ALU.not_equal).then_inc(route.sem, 1)
                dve.wait_ge(route.sem, route(l, 32))
                v_.tensor_tensor(weight[:], chosen[:], sc[:, :, 0], ALU.mult).then_inc(route.sem, 1)
                dve.wait_ge(route.sem, route(l, 33))
                pick_step = seq(route, l, 33)
                pick_step(v_.tensor_reduce(den[:], weight[:], AX.X, ALU.add))
                pick_step(v_.reciprocal(den[:], den[:]))
                for t in range(T):
                    v_.tensor_scalar(weight[:, t], weight[:, t], den[:, t:t + 1], ROUTED_SCALE, ALU.mult, ALU.mult).then_inc(route.sem, 1)
                dve.wait_ge(rank_ps.sem, rank_ps(l, 1))
                ranks = bank[4][:, 0:2 * N_E].rearrange("p (t e) -> p t e", t=T)
                v_.scalar_tensor_tensor(rank[:, :, 0:N_E], chosen[:], FAR, ranks, ALU.mult, ALU.add).then_inc(route.sem, 1)
                v_.tensor_reduce(most[:], bank[4][:, 2 * N_E:3 * N_E], AX.X, ALU.max).then_inc(route.sem, 1)
                dve.wait_ge(route.sem, route(l, 39))
                for r in range(1, MAX_ROUNDS):
                    v_.tensor_scalar(rank[:, :, r * N_E:(r + 1) * N_E], rank[:, :, 0:N_E], float(CAP * r), None, ALU.subtract).then_inc(route.sem, 1)
                v_.memset(rank[:, :, MAX_ROUNDS * N_E:], 0.0).then_inc(route.sem, 1)
                v_.tensor_scalar(over[:, 0:MAX_ROUNDS - 1], tb("thresh"), most[:, 0:1], None, ALU.is_lt).then_inc(route.sem, 1)
                dve.wait_ge(route.sem, route(l, 44))
                v_.tensor_reduce(most[:], over[:, 0:MAX_ROUNDS - 1], AX.X, ALU.add).then_inc(route.sem, 1)
                dve.wait_ge(route.sem, route(l, 45))
                v_.tensor_scalar(rounds_i[:], most[:], 1.0, None, ALU.add).then_inc(rounds_ready.sem, 1)

                def build_pick(n):
                    r4 = rank[:].rearrange("p t (q e) -> p t q e", e=QUAD)
                    for t in range(T):
                        ins = v_.tensor_tensor(pick[:, t], tb("slot").unsqueeze(1).to_broadcast([P, QUAD, CAP]),
                                               r4[:, t, n].unsqueeze(2).to_broadcast([P, QUAD, CAP]), ALU.is_equal)
                    ins.then_inc(picked, 1)

                build_pick(0)
                dve.wait_ge(sh_sg.sem, sh_sg(l, 1))
                v_.tensor_tensor(shared_t, bank[6][:, :], shared_sg, ALU.mult).then_inc(sh_h.sem, 1)
                dve.wait_ge(sh_ps.sem, sh_ps(l, 2))
                dve.wait_ge(sh_h.sem, sh_h(l, 1))
                v_.tensor_tensor(m_h_shared, bank[7][:, :].rearrange("p (j s) -> p j s", j=2), shared_t.rearrange("p (j s) -> p j s", j=2), ALU.mult).then_inc(sh_h.sem, 1)
                wait_alone(dve, rounds_ready, l, 1)
                rounds = dve.value_load(rounds_i[0:1, 0:1], min_val=1, max_val=MAX_ROUNDS)
                q_first = dve.snap(quads)
                with dve.Fori(0, rounds * NQ) as n:
                    q = q_first + n
                    for g in (0, 2):
                        dve.wait_ge(gathered, 4 * q + g + 1)
                        v_.tensor_copy(xg[:, 2 * g:2 * g + 2].rearrange("p k s -> p (k s)"), bank[4][:, :]).then_inc(xg_dve, 1)
                    dve.wait_ge(gathered, 4 * q + 4)
                    dve.wait_ge(picked_w, q + 1)
                    build_pick(n + 1)

                    def hidden(X):
                        dve.wait_ge(h_sg, 2 * q + X + 1)
                        v_.tensor_tensor(m_t[:, X], bank[6 + X][:, 0:FE], m_sg[:, X], ALU.mult).then_inc(h_t, 1)
                        dve.wait_ge(h_t, 2 * q + X + 1)
                        v_.tensor_tensor(m_h[:, X].rearrange("p j q -> p q j"), bank[6 + X][:, FE:2 * FE].rearrange("p (q j) -> p q j", j=2),
                                         m_t[:, X].rearrange("p (q j) -> p q j", j=2), ALU.mult).then_inc(h_done, 1)

                    hidden(0)
                    dve.wait_ge(pick_t_ps, q + 2)
                    v_.tensor_scalar(pick_t[:].rearrange("p a s -> p (a s)"), bank[4][:, :], 0.0, None, ALU.is_gt).then_inc(pick_t_done, 1)
                    v_.tensor_reduce(slot_gate[:], bank[4][:, :].rearrange("p (a s) -> p a s", a=2), AX.X, ALU.add).then_inc(pick_t_done, 1)
                    hidden(1)
                    for X in range(2):
                        for half in range(2):
                            dve.wait_ge(y_hi_done, 4 * q + 2 * X + half + 1)
                            v_.scalar_tensor_tensor(y_lo[:, half], bank[6 + half][:, :], slot_gate[:, X:X + 1], y_hi[:, half].bitcast(F32),
                                                    ALU.mult, ALU.subtract).then_inc(y_lo_done, 1)
                dve.reg_add(quads, quads, rounds * NQ)
                dve.wait_ge(added, dve.snap(quads))
                for t in range(T):
                    for half in range(2):
                        z = x_tok[:, t, half * 512:(half + 1) * 512]
                        ins = v_.scalar_tensor_tensor(z, z, ALPHA, bank[2 * t + half][:, :], ALU.mult, ALU.add)
                ins.then_inc(route.sem, 1)
                dve.wait_ge(route.sem, route(l, 46))
                norm(l, 1, None)


def kernel(**inputs):
    import numpy as _np
    import concourse.bacc as _bacc
    from concourse import mybir as _mybir
    from concourse.bass_utils import run_bass_kernel_spmd as _run

    nc = _bacc.Bacc("TRN2", target_bir_lowering=False, num_devices=1)
    arrays, args = {}, {}
    for name in _INS:
        a = shape_tables() if name == "tables" else _np.ascontiguousarray(inputs[name])
        arrays[f"in_{name}_dram"] = a
        args[name] = nc.dram_tensor(f"in_{name}_dram", a.shape, _mybir.dt.from_np(a.dtype), kind="ExternalInput").ap()
    out = nc.dram_tensor("out_dram", [1, S, D], F32, kind="ExternalOutput").ap()
    trunk(nc, out=out, **args)
    return _run(nc, [arrays], core_ids=[0]).results[0]["out_dram"]


_INS = ("x", "positions", "tables", "w_in", "gate_b", "w_branch", "w_out", "pool_w", "pool_scale", "rg_conv_w",
        "rg_conv_b", "rg_wa", "rg_ba", "rg_wx", "rg_bx", "rg_lambda", "ln1_g", "ln1_b", "router_w", "router_bias",
        "exp_w1", "exp_w3", "exp_w2", "sh_w1", "sh_w3", "sh_w2", "ln2_g", "ln2_b")
```

```python
from contextlib import ExitStack

import numpy as np

import concourse.bass as bass
from concourse import mybir

F32 = mybir.dt.float32
R32 = mybir.dt.float32r
I32 = mybir.dt.int32
ALU = mybir.AluOpType
ACT = mybir.ActivationFunctionType
AX = mybir.AxisListType

P = 128
DEPTH, S, D = 2, 256, 1024
T = S // P
KD = D // P
H = 4
BW = H * P
KB = BW // P
CW = 256
PB = 4
RING = 4
Q0C, V0C, G0C, XP0, GL0 = 0, 2 * BW, 3 * BW, 4 * BW, 7 * BW
N_E, FE = 64, 256
E_GROUPS, TOP_GROUPS = 8, 4
CAP = 64
QUAD = 4
NQ = N_E // QUAD
MAX_ROUNDS = S // CAP
ROUTED_SCALE = 2.5
ALPHA = (2 * DEPTH) ** 0.25
LN_EPS, GN_EPS = 1e-5, 1e-6
RG_C = 8.0
FAR = 4096.0
BIG = 1e30
TWO_PI = 2 * np.pi
ROUND = 1.5 * 2.0 ** 23
PI_A = 6.28125
PI_B = float(np.round((TWO_PI - PI_A) * 2 ** 21) / 2 ** 21)
PI_C = TWO_PI - PI_A - PI_B
PI_BELOW = float(np.nextafter(np.float32(np.pi), np.float32(0)))

N_CHUNKS = 6 + 4 + 2 + 2 + 12 + 4
C_QK, C_V, C_G, C_GL, C_OUT = 6, 10, 12, 14, 26
N_PIECES = 72
P_QK, P_V, P_G, P_GL, P_OUT = 12, 20, 24, 28, 64

TAB = {}
_at = 0
for _name, _n in (("ident", P), ("freq", 1), ("sign", 1), ("before", P), ("ones", P), ("mean", P), ("lower", E_GROUPS * E_GROUPS), ("slot", CAP),
                  ("thresh", MAX_ROUNDS - 1), ("decay_in", H * P), ("decay_across", H * P), ("inv_n", H * S)):
    TAB[_name] = (_at, _at + _n)
    _at += _n
TAB_W = _at
TAB_FIRST = TAB["before"][0]
GB, CVW, CVB, BA, BX, LAM, PSC, SP8, NSP8, PAR_W = 0, 24, 40, 44, 48, 52, 56, 60, 64, 68
PAR_ROWS = 60


class Signal:

    def __init__(self, nc, ctx, name, n, credit=0):
        self.sem, self.n, self.credit = ctx.enter_context(nc.semaphore(name)), n, credit

    def __call__(self, layer, k):
        return layer * self.n + (k + self.credit)


def shape_tables():
    t = np.zeros((P, TAB_W), np.float64)
    i = np.arange(P)

    def put(name, a):
        t[:, TAB[name][0]:TAB[name][1]] = a

    put("ident", np.eye(P))
    put("before", i[:, None] < i[None, :])
    put("ones", 1.0)
    put("mean", 1.0 / P)
    g = np.arange(E_GROUPS)
    put("lower", (g[None, :] < g[:, None]).reshape(1, -1))
    put("slot", np.arange(CAP)[None, :] + FAR)
    put("thresh", CAP * np.arange(1, MAX_ROUNDS)[None, :])
    log_g = np.log(1.0 - 2.0 ** (-5.0 - np.arange(H)))
    ahead = i[None, :] - i[:, None]
    scale = P ** -0.5
    put("decay_in", np.concatenate([np.where(ahead >= 0, np.exp(lg * np.maximum(ahead, 0)), 0.0) * scale for lg in log_g], 1))
    put("decay_across", np.concatenate([np.exp(lg * (ahead + P)) * scale for lg in log_g], 1))
    put("inv_n", np.concatenate([1.0 / np.minimum(2 ** (h + 1), np.arange(S) + 1) for h in range(H)])[None, :])
    put("freq", (10000.0 ** (-(i % 64) / 64.0))[:, None])
    put("sign", np.where(i < 64, -1.0, 1.0)[:, None])
    return t.astype(np.float32)


def trunk(nc, x, positions, tables, w_in, gate_b, w_branch, w_out, pool_w, pool_scale, rg_conv_w, rg_conv_b,
          rg_wa, rg_ba, rg_wx, rg_bx, rg_lambda, ln1_g, ln1_b, router_w, router_bias, exp_w1, exp_w3, exp_w2,
          sh_w1, sh_w3, sh_w2, ln2_g, ln2_b, out):
    with ExitStack() as ctx:
        place = [(nc.sbuf_base + 31) // 32 * 32]

        def at(name, shape, dt, offset):
            return nc.alloc_sbuf_tensor_at(name, [P] + shape, dt, offset=offset)

        def keep(name, shape, dt=F32):
            t = at(name, shape, dt, place[0])
            place[0] += (int(np.prod(shape)) * 4 + 31) // 32 * 32
            return t

        w13 = [keep("w13_a", [2, 2, KD * FE]), None]
        raw = keep("raw", [RING, PB, CW])
        shw = at("shw", [2, KD, FE], F32, place[0] - RING * PB * CW * 4)
        w13_spare = at("w13_spare", [2, 2, KD // 2 * FE], F32, place[0] - RING * PB * CW * 4)
        x_tok = keep("x_tok", [T, D])
        xs_hi = keep("xs_hi", [KD, S], R32)
        xs_lo = keep("xs_lo", [KD, S], R32)
        tab = keep("tab", [TAB_W])
        ln_place = place[0]
        lnp = keep("lnp", [2, D])
        shw2 = at("shw2", [2, D], F32, ln_place)
        small_w = at("small_w", [3, H, P], F32, ln_place)
        rw = keep("rw", [KD, N_E])
        parl = keep("parl", [PAR_W])
        rbl = keep("rbl", [1])
        rope_c = keep("rope_c", [S])
        rope_s = keep("rope_s", [S])
        pos_i = keep("pos_i", [S], I32)
        rows = keep("rows", [P])
        lam_t = keep("lam_t", [4, H])
        stats = keep("stats", [T, 4, 6])
        mv = keep("mv", [T, 2])
        sd = keep("sd", [T])
        eps = keep("eps", [2])
        scratch = keep("scratch", [1])
        rounds_i = keep("rounds_i", [1], I32)

        r1 = place[0]
        w13[1] = keep("w13_b", [2, 2, KD * FE])
        UNIT = H * S * 4
        mix = at("mix", [6, 2 * S], F32, r1)
        xp, xr, yr = (mix[:, 2 * i:2 * i + 2].rearrange("p a (h s) -> p (a h) s", s=S) for i in range(3))
        decayed = at("decayed", [2, 512], F32, r1)
        gelu = at("gelu", [H, S], F32, r1 + UNIT)
        conv = at("conv", [H, S], F32, r1 + 3 * UNIT)
        hid = at("hid", [H, S], F32, r1 + 3 * UNIT)
        rg = at("rg", [H, S], F32, r1 + 4 * UNIT)
        ig = at("ig", [H, S], F32, r1 + 5 * UNIT)
        ag = at("ag", [H, S], F32, r1 + 6 * UNIT)
        pooled = at("pooled", [H, S], F32, r1 + 7 * UNIT)
        ret = at("ret", [2, 2 * S], F32, r1 + 7 * UNIT)
        ang = at("ang", [S], F32, r1 + 6 * UNIT)
        turns = at("turns", [2, S], F32, r1 + 6 * UNIT + S * 4)
        reduced = at("reduced", [2, S], F32, r1 + 4 * UNIT)
        r2 = place[0]
        w2 = [keep("w2_a", [2, 2 * D]), keep("w2_b", [2, 2 * D])]
        whi = at("whi", [RING, PB, CW], R32, r2)
        wlo = at("wlo", [RING, PB, CW], R32, r2 + RING * PB * CW * 4)
        r3 = place[0]
        qk = keep("qk", [4, 2 * S])
        val = keep("val", [T, BW])
        gate_g = keep("gate_g", [2, 2 * S])
        pool_b = at("pool_b", [H, S], F32, place[0] - UNIT)
        merged = keep("merged", [4, 2 * S])
        recip_u = at("recip_u", [H, S], F32, place[0] - 2 * UNIT)
        br_hi = keep("br_hi", [2, KB, S], R32)
        br_lo = keep("br_lo", [2, KB, S], R32)
        tmp1 = keep("tmp1", [2 * S])
        tmp2 = keep("tmp2", [2 * S])
        sg = keep("sg", [2 * S])
        end_mixer = place[0]
        place[0] = r3
        xt = keep("xt", [KD, S])
        xg = keep("xg", [KD, QUAD * CAP])
        pick = keep("pick", [T, QUAD, CAP], R32)
        pick_w = keep("pick_w", [T, QUAD, CAP])
        pick_t = keep("pick_t", [2, S], R32)
        y_hi = keep("y_hi", [2, 512], R32)
        y_lo = keep("y_lo", [2, 512], R32)
        m_sg = keep("m_sg", [2, 2 * P])
        m_t = keep("m_t", [2, 2 * P])
        m_h = keep("m_h", [2, 2, P])
        m_ht = keep("m_ht", [2, 2, P])
        slot_gate = keep("slot_gate", [2])
        sc_t = keep("sc_t", [S])
        sc = keep("sc", [T, 2, N_E])
        g8 = keep("g8", [T, E_GROUPS, 8])
        grp = keep("grp", [T, E_GROUPS])
        cmp_a = keep("cmp_a", [T * E_GROUPS, E_GROUPS])
        cmp_b = keep("cmp_b", [T * E_GROUPS, E_GROUPS])
        gmask = keep("gmask", [T, E_GROUPS])
        gpen = keep("gpen", [T, E_GROUPS])
        masked = keep("masked", [T, N_E])
        best = keep("best", [T, 8])
        taken = keep("taken", [T, N_E])
        chosen = keep("chosen", [T, N_E])
        weight = keep("weight", [T, N_E])
        den = keep("den", [T])
        rank = keep("rank", [T, (MAX_ROUNDS * N_E + QUAD)])
        most = keep("most", [1])
        over = keep("over", [MAX_ROUNDS])
        shared_sg, shared_t = m_sg[:].rearrange("p a s -> p (a s)"), m_t[:].rearrange("p a s -> p (a s)")
        shared_h = at("shared_h", [2, S], F32, r3)
        assert max(end_mixer, place[0]) <= nc.sbuf_usable_end, (end_mixer, place[0], nc.sbuf_usable_end)

        bank = [ctx.enter_context(nc.psum_tensor(f"bank{i}", [P, 512], F32)) for i in range(8)]

        def tb(name):
            return tab[:, TAB[name][0]:TAB[name][1]]

        ident, ones = tb("ident"), tb("ones")

        def plain(name):
            return ctx.enter_context(nc.semaphore(name))

        def sig(name, n, credit=0):
            return Signal(nc, ctx, name, n, credit)

        pos_in, first_in, x_in, tab_in = plain("pos_in"), plain("first_in"), [plain("x_in0"), plain("x_in1")], plain("tab_in")
        rows_ps, start_dve = sig("rows_ps", 1), plain("start_dve")
        rope, rope_act, rope_signed, softplus, softplus_act = sig("rope", 11), sig("rope_act", 2), sig("rope_signed", 1), sig("softplus", 16), sig("softplus_act", 1)
        raw_in = [sig(f"raw_in{i}", 16 * N_PIECES // RING) for i in range(RING)]
        hi_done = sig("hi_done", N_PIECES)
        lo_even, lo_odd = sig("lo_even", N_PIECES // 2, 1), sig("lo_odd", N_PIECES // 2, 1)
        used = sig("used", N_PIECES, RING)
        evac = sig("evac", N_CHUNKS, 2)
        par_in, par_ready = sig("par_in", 8 * 16), sig("par_ready", 3)
        xt_ps, xs_hi_done, xs_lo_done = sig("xt_ps", 4), sig("xs_hi_done", 4), sig("xs_lo_done", 4)
        small_in, ln_in, rw_in = sig("small_in", 48), sig("ln_in", 64), sig("rw_in", 16)
        conv_done = sig("conv_done", 16)
        pool_sum = sig("pool_sum", 13)
        rope_m, roped = sig("rope_m", 8), sig("roped", 4, 1)
        ri_ps, r_done, i_done, a_done, u_done = sig("ri_ps", 2), sig("r_done", 4), sig("i_done", 4), sig("a_done", 4), sig("u_done", 4)
        lru, lru_root = sig("lru", 10), sig("lru_root", 1)
        gelu_sq, gelu_arg, gelu_cube, gelu_tanh, gelu_gate = (sig(n, 1) for n in ("gelu_sq", "gelu_arg", "gelu_cube", "gelu_tanh", "gelu_gate"))
        pl_ps, br_hi_done, br_ready = sig("pl_ps", 1), sig("br_hi_done", 6), sig("br_ready", 6)
        g_sg = sig("g_sg", 2)
        sc_ps, decayed_done, o_ps, o_sb, mean_ps = sig("sc_ps", 4), sig("decayed_done", 4), sig("o_ps", 2), sig("o_sb", 2), sig("mean_ps", 2)
        o_dev, o_sq, var_ps, o_sd, o_norm = sig("o_dev", 2), sig("o_sq", 2), sig("var_ps", 2), sig("o_sd", 2), sig("o_norm", 6)
        gates_sg, merge_done = sig("gates_sg", 24), sig("merge_done", 12)
        m_hi_done, m_lo_done = sig("m_hi_done", 4), sig("m_lo_done", 4)
        ln, ln_sd = sig("ln", 26, 3), sig("ln_sd", 2)
        xt2_ps, xt2_dve, xt2_act, tok_hi, tok_lo = sig("xt2_ps", 4), sig("xt2_dve", 2), sig("xt2_act", 2), sig("tok_hi", 2), sig("tok_lo", 2)
        logit_ps, sig_t, biased_t, sc_tok_ps = sig("logit_ps", 1, 1), sig("sig_t", 1), sig("biased_t", 1), sig("sc_tok_ps", 1)
        route, rank_ps = sig("route", 47), sig("rank_ps", 1)
        rounds_ready = sig("rounds_ready", 1)
        sh_in, sh2_in, sh_ps, sh_sg, sh_h, sh_done = sig("sh_in", 32), sig("sh2_in", 16), sig("sh_ps", 2), sig("sh_sg", 1), sig("sh_h", 2), sig("sh_done", 1)
        w13_in = [[plain(f"w13_in_{p}{h}") for h in range(2)] for p in "ab"]
        w2_in = [[plain(f"w2_in_{p}{h}") for h in range(2)] for p in "ab"]
        picked, picked_w, gathered = plain("picked"), plain("picked_w"), plain("gathered")
        xg_dve, xg_act = plain("xg_dve"), plain("xg_act")
        up_first = [plain("up_first_a"), plain("up_first_b")]
        up_done = [plain("up_done_a"), plain("up_done_b")]
        pick_t_ps, pick_t_done = plain("pick_t_ps"), plain("pick_t_done")
        h_sg, h_t, h_done, ht_ps, ht_done = plain("h_sg"), plain("h_t"), plain("h_done"), plain("ht_ps"), plain("ht_done")
        y_ps, y_hi_done, y_lo_done = plain("y_ps"), plain("y_hi_done"), plain("y_lo_done")
        added = [plain("added_left"), plain("added_right")]
        table_loaded = sig("table_loaded", 1, 1)
        passed = {eng: plain(f"passed_{i}") for i, eng in enumerate((nc.sync, nc.tensor, nc.scalar, nc.gpsimd, nc.vector))}
        out_sem = plain("out_done")

        block = ctx.enter_context(nc.Block())

        def wait_alone(eng, signal, l, k):
            eng.wait_ge(signal.sem, signal(l, k))
            eng.sem_inc(passed[eng], 1)

        def lo_part(eng, vec, l, a, n=0, i=0):
            s = a % RING
            eng.wait_ge(hi_done.sem, hi_done(l, a + 1 + n * i))
            which = (lo_even, lo_odd)[a % 2]
            vec.tensor_tensor(wlo[:, s], raw[:, s], whi[:, s].bitcast(F32), ALU.subtract).then_inc(which.sem, 1)

        @block.sync
        def _(sp):
            sp.dma_start(tab[:, 0:TAB_FIRST], tables[:, 0:TAB_FIRST]).then_inc(first_in, 16)
            for t in range(T):
                sp.dma_start(x_tok[:, t], x[0, t * P:(t + 1) * P, :]).then_inc(x_in[t], 16)

            def piece(l, source, a, n=0, i=0):
                s = a % RING
                which = (lo_even, lo_odd)[a % 2]
                sp.wait_ge(which.sem, which(l, max((a - RING) // 2 + 1, 0) + (n // 2) * i))
                sp.sem_inc(passed[nc.sync], 1)
                sp.dma_start(raw[:, s], source).then_inc(raw_in[s].sem, 16)

            def in_piece(l, col, half):
                return w_in[l].rearrange("(q k) c -> q k c", k=KD)[:, half * PB:(half + 1) * PB, bass.ds(col, CW)]

            quads = sp.alloc_register("quads_before")
            sp.reg_mov(quads, 0)
            with sp.Fori(0, DEPTH) as l:
                for a in range(RING):
                    piece(l, in_piece(l, XP0 + (a // 2) * CW, a % 2), a)
                sp.wait_ge(ln.sem, ln(l, 0))
                sp.wait_ge(start_dve, 3)
                for row, src in ((GB, gate_b[l].rearrange("b (n c) -> (b n) c", c=P)),
                                 (CVW, rg_conv_w[l].rearrange("k (n c) -> (k n) c", c=P)),
                                 (CVB, rg_conv_b[l].rearrange("(n c) -> n c", c=P)),
                                 (BA, rg_ba[l].rearrange("(n c) -> n c", c=P)),
                                 (BX, rg_bx[l].rearrange("(n c) -> n c", c=P)),
                                 (LAM, rg_lambda[l].rearrange("(n c) -> n c", c=P)),
                                 (PSC, pool_scale[l].rearrange("(n c) -> n c", c=P))):
                    sp.dma_start(rows[row:row + src.shape[0], :], src).then_inc(par_in.sem, 16)
                with nc.allow_non_contiguous_dma(reason="one value per partition"):
                    sp.dma_start(rbl[0:N_E, :], router_bias[bass.ds(l, 1)].rearrange("l e -> e l")).then_inc(par_in.sem, 16)
                for j, w in enumerate((pool_w, rg_wa, rg_wx)):
                    sp.dma_start(small_w[:, j], w[l].rearrange("n c e -> c n e")).then_inc(small_in.sem, 16)
                sp.wait_ge(logit_ps.sem, logit_ps(l, 0))
                sp.dma_start(rw[:], router_w[l].rearrange("(q k) e -> q k e", k=KD)).then_inc(rw_in.sem, 16)
                for a in range(RING, P_QK):
                    piece(l, in_piece(l, XP0 + (a // 2) * CW, a % 2), a)
                q_first = sp.snap(quads)

                def up_half(X, h, e):
                    part = slice(h * KD // 2 * FE, (h + 1) * KD // 2 * FE)
                    for m, w in enumerate((exp_w1, exp_w3)):
                        sp.dma_start(w13[X][:, m, :, part], w[l, bass.ds(e, 2)].rearrange("e (q k) f -> q e (k f)", k=KD)[:, :, part]).then_inc(w13_in[X][h], 16)

                sp.wait_ge(up_done[0], q_first + 1)
                up_half(0, 0, 0)
                with sp.Fori(0, 2) as i:
                    for u in range(4):
                        piece(l, in_piece(l, Q0C + (u // 2) * CW + 2 * CW * i, u % 2), P_QK + u, 4, i)
                for u in range(4):
                    piece(l, in_piece(l, V0C + (u // 2) * CW, u % 2), P_V + u)
                for u in range(4):
                    piece(l, in_piece(l, G0C + (u // 2) * CW, u % 2), P_G + u)
                sp.wait_ge(pl_ps.sem, pl_ps(l, 1))
                sp.wait_ge(ri_ps.sem, ri_ps(l, 2))
                sp.dma_start(lnp[:, 0], ln1_g[bass.ds(l, 1)].to_broadcast([P, D])).then_inc(ln_in.sem, 16)
                sp.dma_start(lnp[:, 1], ln1_b[bass.ds(l, 1)].to_broadcast([P, D])).then_inc(ln_in.sem, 16)

                def gl_pieces(j, b, v):
                    a = P_GL + 12 * j + 3 * v
                    for half in range(2):
                        piece(l, in_piece(l, GL0 + v * CW + D * b, half), a + half)
                    piece(l, w_branch[l, b].rearrange("(k q) c -> q k c", q=P)[:, :, v * CW:(v + 1) * CW], a + 2)

                for v in range(4):
                    gl_pieces(0, 1, v)
                    if v == 1:
                        up_half(0, 1, 0)
                for v in range(4):
                    gl_pieces(1, 2, v)
                sp.wait_ge(up_done[1], q_first + 1)
                wait_alone(sp, br_ready, l, 6)
                for v in range(4):
                    gl_pieces(2, 0, v)
                    if v % 2 == 0:
                        up_half(1, v // 2, 2)
                for a in range(8):
                    piece(l, w_out[l].rearrange("(k q) c -> q k c", q=P)[:, (a % 2) * PB:(a % 2 + 1) * PB,
                                                                       (a // 2) * CW:(a // 2 + 1) * CW], P_OUT + a)

                def down_load(X, e):
                    for half in range(2):
                        cols = slice(half * 512, (half + 1) * 512)
                        for one in range(2):
                            sp.dma_start(w2[X][:, one].rearrange("p (j d) -> p j d", j=2)[:, :, cols],
                                         exp_w2[l, bass.ds(e + one, 1)].rearrange("e (q j) d -> q (e j) d", j=2)[:, :, cols]).then_inc(w2_in[X][half], 16)

                sp.wait_ge(lo_even.sem, lo_even(l, N_PIECES // 2))
                sp.wait_ge(lo_odd.sem, lo_odd(l, N_PIECES // 2))
                for j, w in enumerate((sh_w1, sh_w3)):
                    sp.dma_start(shw[:, j], w[l].rearrange("(q k) f -> q k f", k=KD)).then_inc(sh_in.sem, 16)
                sp.wait_ge(used.sem, used(l, N_PIECES))
                down_load(0, 0)
                down_load(1, 2)
                sp.wait_ge(ln.sem, ln(l, 15))
                sp.dma_start(shw2[:], sh_w2[l].rearrange("(j q) d -> q j d", q=P)).then_inc(sh2_in.sem, 16)

                def second_pair_and_down(q, e):
                    sp.wait_ge(up_first[1], q + 1)
                    up_half(1, 0, e + 2)
                    sp.wait_ge(up_done[1], q + 1)
                    up_half(1, 1, e + 2)
                    sp.wait_ge(y_ps, 4 * q - 2)
                    down_load(0, e)
                    sp.wait_ge(y_ps, 4 * q)
                    down_load(1, e + 2)

                sp.wait_ge(sh_ps.sem, sh_ps(l, 2))
                for m, w in enumerate((exp_w1, exp_w3)):
                    sp.dma_start(w13_spare[:, m], w[l, QUAD:QUAD + 2].rearrange("e (q k) f -> q e (k f)", k=KD)[:, :, KD // 2 * FE:]).then_inc(w13_in[0][1], 16)
                wait_alone(sp, rounds_ready, l, 1)
                rounds = sp.value_load(rounds_i[0:1, 0:1], min_val=1, max_val=MAX_ROUNDS)
                sp.wait_ge(up_first[0], q_first + 2)
                up_half(0, 0, QUAD)
                second_pair_and_down(q_first + 1, QUAD)
                with sp.Fori(2, rounds * NQ) as n:
                    q = q_first + n
                    e = (n % NQ) * QUAD
                    sp.wait_ge(up_first[0], q + 1)
                    up_half(0, 0, e)
                    sp.wait_ge(up_done[0], q + 1)
                    up_half(0, 1, e)
                    second_pair_and_down(q, e)
                sp.wait_ge(sh_done.sem, sh_done(l, 1))
                sp.dma_start(lnp[:, 0], ln2_g[bass.ds(l, 1)].to_broadcast([P, D])).then_inc(ln_in.sem, 16)
                sp.dma_start(lnp[:, 1], ln2_b[bass.ds(l, 1)].to_broadcast([P, D])).then_inc(ln_in.sem, 16)
                sp.reg_add(quads, quads, rounds * NQ)
            for t in range(T):
                sp.wait_ge(ln.sem, ln(DEPTH, 2 * t - 2))
                sp.dma_start(out[0, t * P:(t + 1) * P, :], x_tok[:, t]).then_inc(out_sem, 16)
            sp.wait_ge(out_sem, T * 16)

        @block.tensor
        def _(pe):
            def split3(o, a_hi, a_lo, b_hi, b_lo, start, stop):
                nc.tensor.matmul(o, a_lo, b_hi, start=start, stop=False, skip_group_check=True)
                nc.tensor.matmul(o, a_hi, b_lo, start=False, stop=False, skip_group_check=True)
                return nc.tensor.matmul(o, a_hi, b_hi, start=False, stop=stop, skip_group_check=True)

            def blocks(x):
                return lambda kk: x[:, kk]

            def merged_blocks(x):
                return lambda kk: x[:, (kk // 4 + 1) % 2, kk % 4]

            def wait_piece(l, a, n=0, i=0):
                which = (lo_even, lo_odd)[a % 2]
                pe.wait_ge(which.sem, which(l, a // 2 + 1 + (n // 2) * i))

            def chunk_rows(l, a, n, i, b_hi, b_lo, to, first, last):
                s = a % RING
                wait_piece(l, a, n, i)
                for m in range(2):
                    for k in range(PB):
                        mm = split3(to[:, m * S:(m + 1) * S], whi[:, s, k, m * P:(m + 1) * P], wlo[:, s, k, m * P:(m + 1) * P],
                                    b_hi[:, k], b_lo[:, k], first and m == 0 and k == 0, last and k == PB - 1)
                mm.then_inc(used.sem, 1)

            def wide(l, c, a, n=0, i=0, cn=0, second=None):
                pe.wait_ge(evac.sem, evac(l, c - 1 + cn * i))
                for half in range(2):
                    if half and second:
                        second()
                    chunk_rows(l, a + half, n, i, xs_hi[:, half * PB:(half + 1) * PB],
                               xs_lo[:, half * PB:(half + 1) * PB], bank[c % 2], half == 0, half == 1)

            def tall(l, c, a, lhs_hi, lhs_lo, second=None):
                pe.wait_ge(evac.sem, evac(l, c - 1))
                for half in range(2):
                    s = (a + half) % RING
                    if half and second:
                        second()
                    wait_piece(l, a + half)
                    for t in range(T):
                        for k in range(PB):
                            kk = half * PB + k
                            mm = split3(bank[c % 2][:, t * CW:(t + 1) * CW], lhs_hi(kk)[:, t * P:(t + 1) * P],
                                        lhs_lo(kk)[:, t * P:(t + 1) * P], whi[:, s, k], wlo[:, s, k],
                                        half == 0 and t == 0 and k == 0, half == 1 and k == PB - 1)
                    mm.then_inc(used.sem, 1)

            def turn_x(l, done, steps):
                for t in range(T):
                    pe.wait_ge(ln.sem, ln(l, steps - 2 + 2 * t))
                    pe.wait_ge(x_in[t], 16)
                    pe.wait_ge(first_in, 16)
                    for kk in range(4):
                        for k in range(2):
                            mm = nc.tensor.transpose(bank[4 + kk][:, k * S + t * P:k * S + (t + 1) * P],
                                                     x_tok[:, t].rearrange("p (q k) -> p k q", k=KD)[:, 2 * kk + k], ident)
                        if t == T - 1:
                            mm.then_inc(done.sem, 1)

            pe.sem_inc(used.sem, used.credit)
            pe.sem_inc(logit_ps.sem, logit_ps.credit)
            for free in (*up_first, *up_done, pick_t_ps):
                pe.sem_inc(free, 1)
            quads = pe.alloc_register("quads_before")
            pe.reg_mov(quads, 0)
            with pe.Fori(0, DEPTH) as l:
                turn_x(l, xt_ps, 0)
                pe.wait_ge(xs_lo_done.sem, xs_lo_done(l, 2))
                wide(l, 0, 0, second=lambda: pe.wait_ge(xs_lo_done.sem, xs_lo_done(l, 4)))
                wide(l, 1, 2)
                pe.wait_ge(par_in.sem, par_in(l, 8 * 16))
                nc.tensor.transpose(bank[3][:, 0:P], rows[:], ident).then_inc(rows_ps.sem, 1)
                for c in range(2, 5):
                    wide(l, c, 2 * c)
                pe.wait_ge(par_ready.sem, par_ready(l, 1))
                wide(l, 5, 10)
                with pe.Fori(0, 2) as i:
                    for u in range(2):
                        wide(l, C_QK + u, P_QK + 2 * u, 4, i, 2)
                pe.wait_ge(small_in.sem, small_in(l, 48))
                pe.wait_ge(conv_done.sem, conv_done(l, 16))
                for j in range(2):
                    for h in range(H):
                        mm = nc.tensor.matmul(bank[4 + 2 * j + h // 2][:, (h % 2) * S:(h % 2 + 1) * S], small_w[:, 1 + j, h],
                                              conv[:, h], start=True, stop=True)
                    mm.then_inc(ri_ps.sem, 1)
                tall(l, C_V, P_V, blocks(xs_hi), blocks(xs_lo))
                pe.wait_ge(pool_sum.sem, pool_sum(l, 13))
                for h in range(H):
                    mm = nc.tensor.matmul(bank[2 + h // 2][:, (h % 2) * S:(h % 2 + 1) * S], small_w[:, 0, h], pooled[:, h],
                                          start=True, stop=True)
                mm.then_inc(pl_ps.sem, 1)
                tall(l, C_V + 1, P_V + 2, blocks(xs_hi), blocks(xs_lo))

                def scores(h):
                    q, k = qk[:, h // 2, (h % 2) * S:(h % 2 + 1) * S], qk[:, 2 + h // 2, (h % 2) * S:(h % 2 + 1) * S]
                    nc.tensor.matmul(bank[4 + h % 2][:, 0:S], k[:, 0:P], q, start=True, stop=True)
                    nc.tensor.matmul(bank[4 + h % 2][:, S:S + P], k[:, P:S], q[:, P:S], start=True, stop=True).then_inc(sc_ps.sem, 1)

                def mix_values(h):
                    v, to = val[:, :, h * P:(h + 1) * P], bank[6 + h // 2][:, (h % 2) * S:(h % 2 + 1) * S]
                    nc.tensor.matmul(to, v[:, 0], decayed[:, h % 2, 0:S], start=h % 2 == 0, stop=False, skip_group_check=True)
                    return nc.tensor.matmul(to[:, P:S], v[:, 1], decayed[:, h % 2, S:S + P], start=False, stop=True, skip_group_check=True)

                pe.wait_ge(tab_in, 16)
                pe.wait_ge(roped.sem, roped(l, 4))
                pe.wait_ge(i_done.sem, i_done(l, 4))
                scores(0)
                scores(1)
                wide(l, C_G, P_G)
                pe.wait_ge(evac.sem, evac(l, C_V + 2))
                pe.wait_ge(decayed_done.sem, decayed_done(l, 2))
                mix_values(0)
                mix_values(1).then_inc(o_ps.sem, 1)
                scores(2)
                scores(3)
                wide(l, C_G + 1, P_G + 2)
                pe.wait_ge(decayed_done.sem, decayed_done(l, 4))
                mix_values(2)
                mix_values(3).then_inc(o_ps.sem, 1)
                for pair in range(2):
                    pe.wait_ge(o_sb.sem, o_sb(l, pair + 1))
                    nc.tensor.matmul(bank[4 + pair][:, :], tb("mean"), ret[:, pair], start=True, stop=True).then_inc(mean_ps.sem, 1)

                def gates_chunk(j, v, b_hi, b_lo, i):
                    c = C_GL + v
                    pe.wait_ge(evac.sem, evac(l, c - 1 + 4 * i))
                    a = P_GL + 3 * v
                    for half in range(2):
                        chunk_rows(l, a + half, 12, i, xs_hi[:, half * PB:(half + 1) * PB],
                                   xs_lo[:, half * PB:(half + 1) * PB], bank[c % 2], half == 0, half == 1)
                    chunk_rows(l, a + 2, 12, i, b_hi, b_lo, bank[2 + c % 2], True, True)

                pe.wait_ge(br_ready.sem, br_ready(l, 4))
                for v in range(4):
                    gates_chunk(0, v, br_hi[:, 0], br_lo[:, 0], 0)
                    if v < 2:
                        pe.wait_ge(o_sq.sem, o_sq(l, v + 1))
                        nc.tensor.matmul(bank[6 + v][:, :], tb("mean"), (tmp1, tmp2)[v][:], start=True, stop=True).then_inc(var_ps.sem, 1)
                with pe.Fori(1, 3) as j:
                    pe.wait_ge(br_ready.sem, br_ready(l, 4 + j))
                    for v in range(4):
                        gates_chunk(j, v, br_hi[:, j % 2], br_lo[:, j % 2], j)
                pe.wait_ge(m_lo_done.sem, m_lo_done(l, 2))
                for o in range(4):
                    tall(l, C_OUT + o, P_OUT + 2 * o, merged_blocks(br_hi), merged_blocks(br_lo),
                         (lambda: pe.wait_ge(m_lo_done.sem, m_lo_done(l, 4))) if o == 0 else None)

                turn_x(l, xt2_ps, 15)
                pe.wait_ge(rw_in.sem, rw_in(l, 16))
                for k in range(KD):
                    if k % 2 == 0:
                        turned = (xt2_dve, xt2_act)[k // 2 % 2]
                        pe.wait_ge(turned.sem, turned(l, k // 4 + 1))
                    mm = nc.tensor.matmul(bank[4][0:N_E, 0:S], rw[:, k], xt[:, k], start=k == 0, stop=k == KD - 1)
                mm.then_inc(logit_ps.sem, 1)
                pe.wait_ge(sh_in.sem, sh_in(l, 32))

                def shared_up(m, j):
                    for k in range(KD):
                        mm = nc.tensor.matmul(bank[6 + m][:, j * S:(j + 1) * S], shw[:, m, k, j * P:(j + 1) * P], xt[:, k],
                                              start=k == 0, stop=k == KD - 1)
                    return mm

                shared_up(0, 0)
                pe.wait_ge(biased_t.sem, biased_t(l, 1))
                for t in range(T):
                    mm = nc.tensor.transpose(bank[5][:, t * P:(t + 1) * P], sc_t[:, t * P:(t + 1) * P], ident)
                mm.then_inc(sc_tok_ps.sem, 1)
                shared_up(0, 1).then_inc(sh_ps.sem, 1)
                shared_up(1, 0)
                pe.wait_ge(route.sem, route(l, 32))
                nc.tensor.matmul(bank[4][:, 0:N_E], tb("before"), chosen[:, 0], start=True, stop=True)
                nc.tensor.matmul(bank[4][:, N_E:2 * N_E], tb("before"), chosen[:, 1], start=True, stop=False)
                nc.tensor.matmul(bank[4][:, N_E:2 * N_E], ones, chosen[:, 0], start=False, stop=True)
                nc.tensor.matmul(bank[4][:, 2 * N_E:3 * N_E], ones, chosen[:, 0], start=True, stop=False)
                nc.tensor.matmul(bank[4][:, 2 * N_E:3 * N_E], ones, chosen[:, 1], start=False, stop=True).then_inc(rank_ps.sem, 1)
                shared_up(1, 1).then_inc(sh_ps.sem, 1)
                def shared_down(t):
                    for half in range(2):
                        for j in range(2):
                            mm = nc.tensor.matmul(bank[2 * t + half][:, :], shared_h[:, j, t * P:(t + 1) * P],
                                                  shw2[:, j, half * 512:(half + 1) * 512], start=False, stop=False, skip_group_check=True)
                    return mm

                wait_alone(pe, rounds_ready, l, 1)
                rounds = pe.value_load(rounds_i[0:1, 0:1], min_val=1, max_val=MAX_ROUNDS)
                q_first = pe.snap(quads)
                wait_alone(pe, tok_lo, l, 2)
                def quad(q, opens=False, adds_shared=False, spare=False):
                    pe.wait_ge(picked, q + l + 1)
                    for g in range(4):
                        if g == 2:
                            pe.wait_ge(xg_dve, 2 * q + 1)
                        if g == 3:
                            pe.wait_ge(xg_act, 2 * q + 1)
                        for k in range(2):
                            o = bank[4 + g % 2][:, k * S:(k + 1) * S]
                            for t in range(T):
                                for part, x_part in enumerate((xs_lo, xs_hi)):
                                    lhs = x_part[:].rearrange("p k s -> p (k s)")[:, t * D + (2 * g + k) * P:t * D + (2 * g + k + 1) * P]
                                    mm = nc.tensor.matmul(o, lhs, pick[:, t].rearrange("p e c -> p (e c)"),
                                                          start=t == 0 and part == 0, stop=t == 1 and part == 1)
                        mm.then_inc(gathered, 1)

                    def up(X, between=None):
                        for k in range(KD):
                            if k % (KD // 2) == 0:
                                pe.wait_ge(w13_in[X][k // (KD // 2)], 32 * q + 32)
                            if X == 0 and k % 2 == 0:
                                pe.wait_ge((xg_dve, xg_act)[k // 2 % 2], 2 * q + k // 4 + 1)
                            if k == 4 and between:
                                between()
                            for e in range(2):
                                weights, kw = (w13_spare, k - KD // 2) if spare and X == 0 and k >= KD // 2 else (w13[X], k)
                                mm = nc.tensor.matmul(bank[6 + X][64 * e:64 * e + 64, :], xg[:, k, (2 * X + e) * CAP:(2 * X + e + 1) * CAP],
                                                      weights[:, :, e, kw * FE:(kw + 1) * FE], start=k == 0, stop=k == KD - 1,
                                                      skip_group_check=True)
                            if k == KD // 2 - 1:
                                mm.then_inc(up_first[X], 1)
                        mm.then_inc(up_done[X], 1)

                    def turn_h(X):
                        pe.wait_ge(h_done, 2 * q + X + 1)
                        for j in range(2):
                            mm = nc.tensor.transpose(bank[5][:, X * 2 * P + j * P:X * 2 * P + (j + 1) * P], m_h[:, X, j], ident)
                        mm.then_inc(ht_ps, 1)

                    def down(X, half):
                        pe.wait_ge(w2_in[X][half], 32 * q + 32)
                        for j in range(2):
                            for e in range(2):
                                mm = nc.tensor.matmul(bank[6 + half][64 * e:64 * e + 64, :], m_ht[:, X, j, 64 * e:64 * e + 64],
                                                      w2[X][:, e, j * D + half * 512:j * D + (half + 1) * 512],
                                                      start=j == 0, stop=j == 1, skip_group_check=True)
                        mm.then_inc(y_ps, 1)

                    def add(X, half):
                        pe.wait_ge(y_lo_done, 4 * q + 2 * X + half + 1)
                        for t in range(T):
                            for y in (y_lo, y_hi):
                                mm = nc.tensor.matmul(bank[2 * t + half][:, :], pick_t[:, X, t * P:(t + 1) * P], y[:, half],
                                                      start=opens and X == 0 and y is y_lo, stop=False, skip_group_check=True)
                        return mm

                    if opens:
                        pe.wait_ge(sh_h.sem, sh_h(l, 2))
                    up(0)
                    pe.wait_ge(picked_w, q + 1)
                    for X in range(2):
                        for t in range(T):
                            mm = nc.tensor.transpose(bank[4][:, X * S + t * P:X * S + (t + 1) * P],
                                                     pick_w[:, t, 2 * X:2 * X + 2].rearrange("p e c -> p (e c)"), ident)
                    mm.then_inc(pick_t_ps, 1)
                    up(1, lambda: turn_h(0))
                    if adds_shared:
                        pe.wait_ge(sh2_in.sem, sh2_in(l, 16))
                        shared_down(0)
                        shared_down(1).then_inc(sh_done.sem, 1)
                    pe.wait_ge(ht_done, 2 * q + 1)
                    down(0, 0)
                    turn_h(1)
                    down(0, 1)
                    pe.wait_ge(pick_t_done, 2 * q + 2)
                    add(0, 0)
                    pe.wait_ge(ht_done, 2 * q + 2)
                    down(1, 0)
                    add(0, 1)
                    down(1, 1)
                    add(1, 0).then_inc(added[0], 1)
                    add(1, 1).then_inc(added[1], 1)

                quad(q_first, opens=True)
                quad(q_first + 1, spare=True)
                quad(q_first + 2, adds_shared=True)
                with pe.Fori(3, rounds * NQ) as n:
                    quad(q_first + n)
                pe.reg_add(quads, quads, rounds * NQ)

        @block.scalar
        def _(act):
            def copy_hi(o, i):
                return nc.scalar.activation(o, i, ACT.Copy)

            def hi_part(l, a, n=0, i=0):
                s = a % RING
                act.wait_ge(raw_in[s].sem, raw_in[s](l, 16 * (a // RING + 1) + 4 * n * i))
                act.wait_ge(used.sem, used(l, a + 1 - RING + n * i))
                copy_hi(whi[:, s], raw[:, s]).then_inc(hi_done.sem, 1)

            act.sem_inc(table_loaded.sem, table_loaded.credit)
            act.dma_start(pos_i[:], positions.unsqueeze(0).to_broadcast([P, S])).then_inc(pos_in, 16)
            quads = act.alloc_register("quads_before")
            act.reg_mov(quads, 0)
            with act.Fori(0, DEPTH) as l:
                act.wait_ge(start_dve, 2)
                act.wait_ge(table_loaded.sem, table_loaded(l, 0))
                nc.scalar.activation(scratch[:], eps[:, 0:1], ACT.Sigmoid).then_inc(table_loaded.sem, 1)
                hi_part(l, 0)
                for kk in range(4):
                    act.wait_ge(xt_ps.sem, xt_ps(l, kk + 1))
                    copy_hi(xs_hi[:, 2 * kk:2 * kk + 2].rearrange("p k s -> p (k s)"), bank[4 + kk][:, :]).then_inc(xs_hi_done.sem, 1)
                for a in range(1, 10):
                    hi_part(l, a)
                    if a == 6:
                        act.wait_ge(softplus.sem, softplus(l, 1))
                        nc.scalar.activation(lam_t[:, 1], lam_t[:, 0], ACT.Exp).then_inc(softplus_act.sem, 1)
                    if a == 8:
                        act.wait_ge(rope.sem, rope(l, 11))
                        nc.scalar.activation(rope_c[:], turns[:, 0], ACT.Sin).then_inc(rope_act.sem, 1)
                        nc.scalar.activation(rope_s[:], turns[:, 1], ACT.Sin).then_inc(rope_act.sem, 1)
                for a in range(10, 14):
                    hi_part(l, a)
                with act.Fori(0, 2) as i:
                    for u in range(4):
                        hi_part(l, P_QK + 2 + u, 4, i)
                act.wait_ge(par_ready.sem, par_ready(l, 3))
                act.wait_ge(ri_ps.sem, ri_ps(l, 1))
                for h in range(H):
                    nc.scalar.activation(rg[:, h], bank[4 + h // 2][:, (h % 2) * S:(h % 2 + 1) * S], ACT.Sigmoid,
                                         bias=parl[:, BA + h:BA + h + 1]).then_inc(r_done.sem, 1)
                act.wait_ge(ri_ps.sem, ri_ps(l, 2))
                for h in range(H):
                    nc.scalar.activation(ig[:, h], bank[6 + h // 2][:, (h % 2) * S:(h % 2 + 1) * S], ACT.Sigmoid,
                                         bias=parl[:, BX + h:BX + h + 1]).then_inc(i_done.sem, 1)
                hi_part(l, P_V + 2)
                hi_part(l, P_V + 3)
                act.wait_ge(conv_done.sem, conv_done(l, 16))
                act.wait_ge(evac.sem, evac(l, 6))
                nc.scalar.activation(gelu[:], yr, ACT.Square).then_inc(gelu_sq.sem, 1)
                act.wait_ge(r_done.sem, r_done(l, 4))
                for h in range(H):
                    nc.scalar.activation(ag[:, h], rg[:, h], ACT.Exp, scale=parl[:, NSP8 + h:NSP8 + h + 1]).then_inc(a_done.sem, 1)
                act.wait_ge(a_done.sem, a_done(l, 4))
                for h in range(H):
                    nc.scalar.activation(rg[:, h], rg[:, h], ACT.Tanh, scale=parl[:, SP8 + h:SP8 + h + 1]).then_inc(u_done.sem, 1)
                hi_part(l, P_G)
                hi_part(l, P_G + 1)
                act.wait_ge(pl_ps.sem, pl_ps(l, 1))
                for h in range(H):
                    nc.scalar.activation(br_hi[:, 0, h], bank[2 + h // 2][:, (h % 2) * S:(h % 2 + 1) * S], ACT.Copy,
                                         scale=parl[:, PSC + h:PSC + h + 1]).then_inc(br_hi_done.sem, 1)
                hi_part(l, P_G + 2)
                hi_part(l, P_G + 3)
                act.wait_ge(gelu_cube.sem, gelu_cube(l, 1))
                nc.scalar.activation(gelu[:], gelu[:], ACT.Tanh, scale=0.7978845608028654).then_inc(gelu_tanh.sem, 1)
                act.wait_ge(used.sem, used(l, P_G + 2))
                nc.scalar.activation(sg[:], bank[0][:, :], ACT.Sigmoid).then_inc(g_sg.sem, 1)
                act.wait_ge(o_ps.sem, o_ps(l, 1))
                nc.scalar.activation(ret[:, 0], bank[6][:, :], ACT.Copy).then_inc(o_sb.sem, 1)
                for a in range(3):
                    hi_part(l, P_GL + a)
                act.wait_ge(used.sem, used(l, P_G + 4))
                act.wait_ge(evac.sem, evac(l, C_G + 1))
                nc.scalar.activation(sg[:], bank[1][:, :], ACT.Sigmoid).then_inc(g_sg.sem, 1)
                act.wait_ge(o_ps.sem, o_ps(l, 2))
                nc.scalar.activation(ret[:, 1], bank[7][:, :], ACT.Copy).then_inc(o_sb.sem, 1)
                act.wait_ge(lru.sem, lru(l, 4))
                nc.scalar.activation(rg[:], rg[:], ACT.Sqrt, scale=2.0).then_inc(lru_root.sem, 1)
                for pair in range(2):
                    act.wait_ge(o_dev.sem, o_dev(l, pair + 1))
                    nc.scalar.activation((tmp1, tmp2)[pair][:], ret[:, pair], ACT.Square).then_inc(o_sq.sem, 1)

                def gates(j, v, b, i, first):
                    for a in range(3):
                        hi_part(l, P_GL + 3 * (v + 1) + a, 12, i)
                    act.wait_ge(used.sem, used(l, P_GL + 3 * v + 2 + 12 * i))
                    if first and v == 0:
                        act.wait_ge(evac.sem, evac(l, C_GL))
                    else:
                        act.wait_ge(merge_done.sem, merge_done(l, v + 4 * i))
                    for m in range(2):
                        nc.scalar.activation(sg[:, m * S:(m + 1) * S], bank[v % 2][:, m * S:(m + 1) * S], ACT.Sigmoid,
                                             bias=parl[:, GB + b * KD + 2 * v + m:GB + b * KD + 2 * v + m + 1]).then_inc(gates_sg.sem, 1)

                for v in range(4):
                    gates(0, v, 1, 0, True)
                    if v == 1:
                        act.wait_ge(lru.sem, lru(l, 10))
                        copy_hi(br_hi[:, 1], rg[:]).then_inc(br_hi_done.sem, 1)
                    if v == 2:
                        for pair in range(2):
                            act.wait_ge(var_ps.sem, var_ps(l, pair + 1))
                            nc.scalar.activation((tmp1, tmp2)[pair][:], bank[6 + pair][:, :], ACT.Sqrt, bias=eps[:, 1:2]).then_inc(o_sd.sem, 1)
                act.wait_ge(o_norm.sem, o_norm(l, 6))
                act.wait_ge(used.sem, used(l, P_GL + 12))
                copy_hi(br_hi[:, 0], ret[:].rearrange("p a (k s) -> p (a k) s", s=S)).then_inc(br_hi_done.sem, 1)
                def merged_hi(o):
                    act.wait_ge(merge_done.sem, merge_done(l, 8 + o + 1))
                    act.wait_ge(used.sem, used(l, P_GL + 24 if o < 2 else P_OUT))
                    copy_hi(br_hi[:, 1 - o // 2, 2 * (o % 2):2 * (o % 2) + 2].rearrange("p k s -> p (k s)"), merged[:, o]).then_inc(m_hi_done.sem, 1)

                for j in (1, 2):
                    for v in range(4):
                        gates(j, v, (j + 1) % 3, j, False)
                        if j == 2 and v in (2, 3):
                            merged_hi(v - 2)
                merged_hi(2)
                merged_hi(3)
                for a in range(3, 8):
                    hi_part(l, P_OUT + a)
                act.wait_ge(ln.sem, ln(l, 10))
                nc.scalar.activation(sd[:], mv[:, :, 1], ACT.Sqrt, bias=eps[:, 0:1]).then_inc(ln_sd.sem, 1)
                act.wait_ge(ln.sem, ln(l, 15))
                for kk in (1, 3):
                    act.wait_ge(xt2_ps.sem, xt2_ps(l, kk + 1))
                    nc.scalar.activation(xt[:, 2 * kk:2 * kk + 2].rearrange("p k s -> p (k s)"), bank[4 + kk][:, :], ACT.Copy).then_inc(xt2_act.sem, 1)
                act.wait_ge(logit_ps.sem, logit_ps(l, 1))
                nc.scalar.activation(sc_t[0:N_E, :], bank[4][0:N_E, 0:S], ACT.Sigmoid).then_inc(sig_t.sem, 1)
                for t in range(T):
                    copy_hi(xs_hi[:].rearrange("p k s -> p (k s)")[:, t * D:(t + 1) * D].rearrange("p (k q) -> p k q", k=KD),
                            x_tok[:, t].rearrange("p (q k) -> p k q", k=KD)).then_inc(tok_hi.sem, 1)
                act.wait_ge(sh_ps.sem, sh_ps(l, 1))
                nc.scalar.activation(shared_sg, bank[6][:, :], ACT.Sigmoid).then_inc(sh_sg.sem, 1)
                wait_alone(act, rounds_ready, l, 1)
                rounds = act.value_load(rounds_i[0:1, 0:1], min_val=1, max_val=MAX_ROUNDS)
                q_first = act.snap(quads)
                with act.Fori(0, rounds * NQ) as n:
                    q = q_first + n
                    for g in (1, 3):
                        act.wait_ge(gathered, 4 * q + g + 1)
                        nc.scalar.activation(xg[:, 2 * g:2 * g + 2].rearrange("p k s -> p (k s)"), bank[5][:, :], ACT.Copy).then_inc(xg_act, 1)

                    def act_h(X):
                        act.wait_ge(up_done[X], q + 2)
                        nc.scalar.activation(m_sg[:, X], bank[6 + X][:, 0:FE], ACT.Sigmoid).then_inc(h_sg, 1)

                    def ht_out(X):
                        act.wait_ge(ht_ps, 2 * q + X + 1)
                        nc.scalar.activation(m_ht[:, X].rearrange("p j s -> p (j s)"), bank[5][:, X * 2 * P:(X + 1) * 2 * P], ACT.Copy).then_inc(ht_done, 1)

                    def y_out(X, half):
                        act.wait_ge(y_ps, 4 * q + 2 * X + half + 1)
                        nc.scalar.activation(y_hi[:, half], bank[6 + half][:, :], ACT.Copy, scale=slot_gate[:, X:X + 1]).then_inc(y_hi_done, 1)

                    act_h(0)
                    ht_out(0)
                    act_h(1)
                    act.wait_ge(pick_t_done, 2 * q + 2)
                    y_out(0, 0)
                    ht_out(1)
                    y_out(0, 1)
                    y_out(1, 0)
                    y_out(1, 1)
                act.reg_add(quads, quads, rounds * NQ)
                act.wait_ge(ln.sem, ln(l, 21))
                nc.scalar.activation(sd[:], mv[:, :, 1], ACT.Sqrt, bias=eps[:, 0:1]).then_inc(ln_sd.sem, 1)

        @block.gpsimd
        def _(pool):
            g = nc.gpsimd
            pool.sem_inc(lo_even.sem, lo_even.credit)
            pool.wait_ge(x_in[1], 16)
            pool.dma_start(tab[:, TAB_FIRST:], tables[:, TAB_FIRST:]).then_inc(tab_in, 16)
            quads = pool.alloc_register("quads_before")
            pool.reg_mov(quads, 0)
            with pool.Fori(0, DEPTH) as l:
                lo_part(pool, g, l, 0)
                with pool.Fori(0, 2) as i:
                    for u in (2, 4):
                        lo_part(pool, g, l, u, 4, i)
                count = [0]

                def step(ins):
                    count[0] += 1
                    ins.then_inc(pool_sum.sem, 1)
                    wait_alone(pool, pool_sum, l, count[0])

                pool.wait_ge(evac.sem, evac(l, 2))
                step(g.tensor_tensor(pooled[:, :, 1:], xp[:, :, 1:], xp[:, :, :-1], ALU.add))
                lo_part(pool, g, l, 10)
                step(g.tensor_copy(pooled[:, :, 0:1], xp[:, :, 0:1]))
                step(g.tensor_tensor(pool_b[:, 1:, 2:], pooled[:, 1:, 2:], pooled[:, 1:, :-2], ALU.add))
                step(g.tensor_copy(pool_b[:, 1:, 0:2], pooled[:, 1:, 0:2]))
                lo_part(pool, g, l, 12)
                step(g.tensor_tensor(pooled[:, 2:, 4:], pool_b[:, 2:, 4:], pool_b[:, 2:, :-4], ALU.add))
                step(g.tensor_copy(pooled[:, 2:, 0:4], pool_b[:, 2:, 0:4]))
                step(g.tensor_tensor(pool_b[:, 3:, 8:], pooled[:, 3:, 8:], pooled[:, 3:, :-8], ALU.add))
                step(g.tensor_copy(pool_b[:, 3:, 0:8], pooled[:, 3:, 0:8]))
                pool.wait_ge(tab_in, 16)
                inv_n = tb("inv_n").rearrange("p (h s) -> p h s", h=H)
                with pool.Fori(0, 2) as i:
                    for u in (2, 4):
                        lo_part(pool, g, l, P_QK + u, 4, i)
                for h in range(H):
                    src = (pooled, pool_b)[h % 2]
                    step(g.tensor_tensor(pooled[:, h], src[:, h], inv_n[:, h], ALU.mult))
                step(g.tensor_tensor(pooled[:], pooled[:], xp, ALU.subtract))
                lo_part(pool, g, l, P_V + 2)
                lo_part(pool, g, l, P_G)
                pool.wait_ge(gelu_arg.sem, gelu_arg(l, 1))
                g.tensor_tensor(gelu[:], gelu[:], yr, ALU.mult).then_inc(gelu_cube.sem, 1)
                lo_part(pool, g, l, P_G + 2)
                lo_part(pool, g, l, P_GL)
                lo_part(pool, g, l, P_GL + 2)
                for a in range(4, 16, 2):
                    lo_part(pool, g, l, P_GL + a)
                with pool.Fori(1, 3) as j:
                    for a in range(4, 16, 2):
                        lo_part(pool, g, l, P_GL + a, 12, j)
                for a in (4, 6):
                    lo_part(pool, g, l, P_OUT + a)
                for t in range(T):
                    pool.wait_ge(tok_hi.sem, tok_hi(l, t + 1))
                    g.tensor_tensor(xs_lo[:].rearrange("p k s -> p (k s)")[:, t * D:(t + 1) * D].rearrange("p (k q) -> p k q", k=KD),
                                    x_tok[:, t].rearrange("p (q k) -> p k q", k=KD),
                                    xs_hi[:].rearrange("p k s -> p (k s)")[:, t * D:(t + 1) * D].rearrange("p (k q) -> p k q", k=KD).bitcast(F32),
                                    ALU.subtract).then_inc(tok_lo.sem, 1)
                wait_alone(pool, rounds_ready, l, 1)
                rounds = pool.value_load(rounds_i[0:1, 0:1], min_val=1, max_val=MAX_ROUNDS)
                q_first = pool.snap(quads)
                with pool.Fori(0, rounds * NQ) as n:
                    q = q_first + n
                    pool.wait_ge(picked, q + l + 1)
                    pool.wait_ge(pick_t_ps, q + 1)
                    gate = weight[:].rearrange("p t (q e) -> p t q e", e=QUAD)
                    for t in range(T):
                        ins = g.tensor_tensor(pick_w[:, t], pick[:, t].bitcast(F32),
                                              gate[:, t, n % NQ].unsqueeze(2).to_broadcast([P, QUAD, CAP]), ALU.mult)
                    ins.then_inc(picked_w, 1)
                pool.reg_add(quads, quads, rounds * NQ)

        @block.vector
        def _(dve):
            v_ = nc.vector

            def seq(signal, l, first=0):
                count = [first]

                def step(ins):
                    count[0] += 1
                    ins.then_inc(signal.sem, 1)
                    dve.wait_ge(signal.sem, signal(l, count[0]))
                return step

            for free in (evac, lo_odd, roped, ln):
                dve.sem_inc(free.sem, free.credit)
            v_.memset(eps[:, 0:1], LN_EPS).then_inc(start_dve, 1)
            v_.memset(eps[:, 1:2], GN_EPS).then_inc(start_dve, 1)
            v_.memset(rows[:], 0.0).then_inc(start_dve, 1)
            def rope_turns(step):
                step(v_.tensor_copy(ang[:], pos_i[:]))
                step(v_.tensor_scalar(ang[:], ang[:], tb("freq"), None, ALU.mult))
                step(v_.tensor_scalar(turns[:, 0], ang[:], 1.0 / TWO_PI, 0.25, ALU.mult, ALU.add))
                step(v_.tensor_scalar(turns[:, 1], ang[:], 1.0 / TWO_PI, None, ALU.mult))
                step(v_.tensor_scalar(turns[:], turns[:], ROUND, None, ALU.add))
                step(v_.tensor_scalar(turns[:], turns[:], ROUND, None, ALU.subtract))

            def rope_reduced(step):
                step(v_.scalar_tensor_tensor(reduced[:], turns[:], -PI_A, ang[:].unsqueeze(1).to_broadcast([P, 2, S]), ALU.mult, ALU.add))
                step(v_.scalar_tensor_tensor(reduced[:], turns[:], -PI_B, reduced[:], ALU.mult, ALU.add))
                step(v_.scalar_tensor_tensor(reduced[:], turns[:], -PI_C, reduced[:], ALU.mult, ALU.add))
                step(v_.tensor_scalar(reduced[:, 0], reduced[:, 0], np.pi / 2, None, ALU.add))
                step(v_.tensor_scalar(turns[:], reduced[:], PI_BELOW, -PI_BELOW, ALU.min, ALU.max))

            def softplus_log(step):
                step(v_.tensor_scalar(lam_t[:, 2], lam_t[:, 1], 2.0, None, ALU.add))
                step(v_.reciprocal(lam_t[:, 2], lam_t[:, 2]))
                step(v_.tensor_tensor(lam_t[:, 1], lam_t[:, 1], lam_t[:, 2], ALU.mult))
                step(v_.tensor_tensor(lam_t[:, 2], lam_t[:, 1], lam_t[:, 1], ALU.mult))
                step(v_.tensor_scalar(lam_t[:, 3], lam_t[:, 2], 1.0 / 17, None, ALU.mult))
                for c in (15, 13, 11, 9, 7, 5, 3):
                    step(v_.scalar_tensor_tensor(lam_t[:, 3], lam_t[:, 3], 1.0 / c, lam_t[:, 2], ALU.add, ALU.mult))
                step(v_.scalar_tensor_tensor(lam_t[:, 3], lam_t[:, 3], 1.0, lam_t[:, 1], ALU.add, ALU.mult))

            def softplus_sum(step):
                step(v_.tensor_scalar(lam_t[:, 2], parl[:, LAM:LAM + H], -1.0, 0.0, ALU.mult, ALU.max))
                step(v_.scalar_tensor_tensor(lam_t[:, 2], lam_t[:, 3], 2.0, lam_t[:, 2], ALU.mult, ALU.add))
                v_.tensor_scalar(parl[:, SP8:SP8 + H], lam_t[:, 2], RG_C, None, ALU.mult).then_inc(par_ready.sem, 1)
                v_.tensor_scalar(parl[:, NSP8:NSP8 + H], lam_t[:, 2], -RG_C, None, ALU.mult).then_inc(par_ready.sem, 1)

            def lo(l, a, n=0, i=0):
                lo_part(dve, v_, l, a, n, i)

            def norm(l, call, parts):
                base = (8, 19)[call]
                wait_alone(dve, ln, l, base)
                for t in range(T):
                    v_.bn_aggr(mv[:, t], stats[:, t, 0:parts].rearrange("p a b -> p (a b)")).then_inc(ln.sem, 1)
                dve.wait_ge(ln_in.sem, ln_in(l, 32 * (call + 1)))
                dve.wait_ge(ln.sem, ln(l, base + 2))
                for t in range(T):
                    v_.scalar_tensor_tensor(x_tok[:, t], x_tok[:, t], mv[:, t, 0:1], lnp[:, 0], ALU.subtract, ALU.mult).then_inc(ln.sem, 1)
                    if t == 0:
                        dve.wait_ge(ln_sd.sem, ln_sd(l, call + 1))
                        v_.reciprocal(sd[:], sd[:]).then_inc(ln.sem, 1)
                    dve.wait_ge(ln.sem, ln(l, base + 4 + 2 * t))
                    v_.scalar_tensor_tensor(x_tok[:, t], x_tok[:, t], sd[:, t:t + 1], lnp[:, 1], ALU.mult, ALU.add).then_inc(ln.sem, 1)

            quads = dve.alloc_register("quads_before")
            dve.reg_mov(quads, 0)
            with dve.Fori(0, DEPTH) as l:
                for kk in range(4):
                    dve.wait_ge(xs_hi_done.sem, xs_hi_done(l, kk + 1))
                    v_.tensor_tensor(xs_lo[:, 2 * kk:2 * kk + 2].rearrange("p k s -> p (k s)"), bank[4 + kk][:, :],
                                     xs_hi[:, 2 * kk:2 * kk + 2].rearrange("p k s -> p (k s)").bitcast(F32), ALU.subtract).then_inc(xs_lo_done.sem, 1)
                lo(l, 1)
                rope_step = seq(rope, l)
                softplus_step = seq(softplus, l)
                for u in range(4):
                    lo(l, 2 * u + 3)
                    if u == 0:
                        dve.wait_ge(pos_in, 16)
                        rope_turns(rope_step)
                    elif u == 1:
                        dve.wait_ge(rows_ps.sem, rows_ps(l, 1))
                        v_.tensor_copy(parl[:, 0:PAR_ROWS], bank[3][:, 0:PAR_ROWS]).then_inc(par_ready.sem, 1)
                        dve.wait_ge(par_ready.sem, par_ready(l, 1))
                        softplus_step(v_.scalar_tensor_tensor(lam_t[:, 0], parl[:, LAM:LAM + H], -1.0, parl[:, LAM:LAM + H], ALU.mult, ALU.min))
                    elif u == 2:
                        rope_reduced(rope_step)
                    else:
                        dve.wait_ge(softplus_act.sem, softplus_act(l, 1))
                        softplus_log(softplus_step)
                        softplus_sum(softplus_step)
                    dve.wait_ge(used.sem, used(l, 2 * u + 2))
                    v_.tensor_copy(mix[:, u], bank[u % 2][:, :]).then_inc(evac.sem, 1)
                dve.wait_ge(evac.sem, evac(l, 4))

                def conv_tap(k):
                    for h in range(H):
                        w = parl[:, CVW + 4 * k + h:CVW + 4 * k + h + 1]
                        if k == 0:
                            v_.tensor_scalar(conv[:, h], xr[:, h], w, parl[:, CVB + h:CVB + h + 1], ALU.mult, ALU.add).then_inc(conv_done.sem, 1)
                        else:
                            dve.wait_ge(conv_done.sem, conv_done(l, 4 * (k - 1) + h + 1))
                            v_.scalar_tensor_tensor(conv[:, h, k:], xr[:, h, :-k], w, conv[:, h, k:], ALU.mult, ALU.add).then_inc(conv_done.sem, 1)

                for u in range(2):
                    lo(l, 11 + 2 * u)
                    conv_tap(2 * u)
                    dve.wait_ge(used.sem, used(l, 8 + 2 * u + 2))
                    v_.tensor_copy(mix[:, 4 + u], bank[u][:, :]).then_inc(evac.sem, 1)
                    conv_tap(2 * u + 1)
                dve.wait_ge(rope_act.sem, rope_act(l, 2))
                v_.tensor_scalar(rope_s[:], rope_s[:], tb("sign"), None, ALU.mult).then_inc(rope_signed.sem, 1)
                wait_alone(dve, rope_signed, l, 1)
                with dve.Fori(0, 2) as i:
                    for u in range(2):
                        lo(l, P_QK + 2 * u + 3, 4, i)
                        dve.wait_ge(used.sem, used(l, P_QK + 2 * u + 2 + 4 * i))
                        dve.wait_ge(roped.sem, roped(l, u + 2 * i))
                        b3 = bank[u][:, :].rearrange("p (h s) -> p h s", h=2)
                        t1, t2 = tmp1[:].rearrange("p (h s) -> p h s", h=2), tmp2[:].rearrange("p (h s) -> p h s", h=2)
                        v_.tensor_tensor(t1, b3, rope_c[:].unsqueeze(1).to_broadcast([P, 2, S]), ALU.mult).then_inc(rope_m.sem, 1)
                        v_.tensor_tensor(t2[0:64], b3[64:128], rope_s[0:64, :].unsqueeze(1).to_broadcast([64, 2, S]), ALU.mult).then_inc(rope_m.sem, 1)
                        v_.tensor_tensor(t2[64:128], b3[0:64], rope_s[64:128, :].unsqueeze(1).to_broadcast([64, 2, S]), ALU.mult).then_inc(evac.sem, 1)
                        dve.wait_ge(rope_m.sem, rope_m(l, 2 * u + 2 + 4 * i))
                        dve.wait_ge(evac.sem, evac(l, C_QK + u + 1 + 2 * i))
                        v_.tensor_tensor(qk[:, bass.ds(u + 2 * i, 1)].rearrange("p a s -> p (a s)"), tmp1[:], tmp2[:], ALU.add).then_inc(roped.sem, 1)

                def values(c):
                    dve.wait_ge(used.sem, used(l, P_V + 2 * c + 2))
                    v_.tensor_copy(val[:, :, c * CW:(c + 1) * CW], bank[c][:, :].rearrange("p (t c) -> p t c", t=T)).then_inc(evac.sem, 1)

                def decay(h):
                    dve.wait_ge(sc_ps.sem, sc_ps(l, h + 1))
                    if h >= 2:
                        dve.wait_ge(o_ps.sem, o_ps(l, 1))
                    else:
                        dve.wait_ge(pool_sum.sem, pool_sum(l, 13))
                    masks = tb("decay_in")[:, h * P:(h + 1) * P], tb("decay_across")[:, h * P:(h + 1) * P]
                    b3 = bank[4 + h % 2]
                    v_.tensor_tensor(decayed[:, h % 2, P:S], b3[:, P:S], masks[1], ALU.mult)
                    v_.tensor_tensor(decayed[:, h % 2, 0:P], b3[:, 0:P], masks[0], ALU.mult)
                    v_.tensor_tensor(decayed[:, h % 2, S:S + P], b3[:, S:S + P], masks[0], ALU.mult).then_inc(decayed_done.sem, 1)

                dve.wait_ge(tab_in, 16)
                lo(l, P_V + 3)
                values(0)
                dve.wait_ge(gelu_sq.sem, gelu_sq(l, 1))
                v_.tensor_scalar(gelu[:], gelu[:], 0.044715, 1.0, ALU.mult, ALU.add).then_inc(gelu_arg.sem, 1)
                chain = seq(lru, l)
                dve.wait_ge(i_done.sem, i_done(l, 4))
                chain(v_.tensor_tensor(ig[:], ig[:], conv[:], ALU.mult))
                lo(l, P_G + 1)
                values(1)
                decay(0)
                decay(1)
                dve.wait_ge(u_done.sem, u_done(l, 4))
                chain(v_.tensor_scalar(recip_u[:], rg[:], 1.0, None, ALU.add))
                chain(v_.reciprocal(recip_u[:], recip_u[:]))
                chain(v_.scalar_tensor_tensor(rg[:], rg[:], 1e-34, recip_u[:], ALU.max, ALU.mult))
                lo(l, P_G + 3)
                for h in range(H):
                    dve.wait_ge(br_hi_done.sem, br_hi_done(l, h + 1))
                    v_.scalar_tensor_tensor(br_lo[:, 0, h], bank[2 + h // 2][:, (h % 2) * S:(h % 2 + 1) * S], parl[:, PSC + h:PSC + h + 1],
                                            br_hi[:, 0, h].bitcast(F32), ALU.mult, ALU.subtract).then_inc(br_ready.sem, 1)
                dve.wait_ge(g_sg.sem, g_sg(l, 1))
                v_.tensor_tensor(gate_g[:, 0], bank[0][:, :], sg[:], ALU.mult).then_inc(evac.sem, 1)
                decay(2)
                decay(3)
                lo(l, P_GL + 1)
                dve.wait_ge(g_sg.sem, g_sg(l, 2))
                v_.tensor_tensor(gate_g[:, 1], bank[1][:, :], sg[:], ALU.mult).then_inc(evac.sem, 1)
                for pair in range(2):
                    dve.wait_ge(mean_ps.sem, mean_ps(l, pair + 1))
                    v_.tensor_tensor(ret[:, pair], ret[:, pair], bank[4 + pair][:, :], ALU.subtract).then_inc(o_dev.sem, 1)
                dve.wait_ge(gelu_tanh.sem, gelu_tanh(l, 1))
                v_.scalar_tensor_tensor(gelu[:], gelu[:], 1.0, yr, ALU.add, ALU.mult).then_inc(gelu_gate.sem, 1)

                def merge(v, i, first):
                    dve.wait_ge(gates_sg.sem, gates_sg(l, 2 * v + 2 + 8 * i))
                    dve.wait_ge(used.sem, used(l, P_GL + 3 * v + 3 + 12 * i))
                    if first:
                        v_.tensor_tensor(merged[:, v], sg[:], bank[2 + v % 2][:, :], ALU.mult).then_inc(evac.sem, 1)
                        dve.wait_ge(evac.sem, evac(l, C_GL + v + 1))
                        dve.sem_inc(merge_done.sem, 1)
                    else:
                        v_.tensor_tensor(sg[:], sg[:], bank[2 + v % 2][:, :], ALU.mult).then_inc(evac.sem, 1)
                        dve.wait_ge(evac.sem, evac(l, C_GL + v + 1 + 4 * i))
                        v_.tensor_tensor(merged[:, v], merged[:, v], sg[:], ALU.add).then_inc(merge_done.sem, 1)

                def lru_scan(h):
                    v_.tensor_tensor_scan(hid[:, h], ag[:, h], ig[:, h], 0.0, ALU.mult, ALU.add).then_inc(lru.sem, 1)

                def unit_norm(pair, k):
                    tmp = (tmp1, tmp2)[pair]
                    if k == 0:
                        dve.wait_ge(o_sd.sem, o_sd(l, pair + 1))
                        v_.reciprocal(tmp[:], tmp[:]).then_inc(o_norm.sem, 1)
                    elif k == 1:
                        dve.wait_ge(o_norm.sem, o_norm(l, pair + 1))
                        v_.tensor_tensor(ret[:, pair], ret[:, pair], tmp[:], ALU.mult).then_inc(o_norm.sem, 1)
                    else:
                        dve.wait_ge(o_norm.sem, o_norm(l, pair + 3))
                        v_.tensor_tensor(ret[:, pair], ret[:, pair], gate_g[:, pair], ALU.mult).then_inc(o_norm.sem, 1)

                lo(l, P_GL + 3)
                lo(l, P_GL + 5)
                dve.wait_ge(lru_root.sem, lru_root(l, 1))
                chain(v_.tensor_tensor(ig[:], rg[:], ig[:], ALU.mult))
                dve.wait_ge(a_done.sem, a_done(l, 4))
                lru_scan(0)
                merge(0, 0, True)
                lo(l, P_GL + 7)
                lru_scan(1)
                lru_scan(2)
                lru_scan(3)
                dve.wait_ge(gelu_gate.sem, gelu_gate(l, 1))
                dve.wait_ge(lru.sem, lru(l, 9))
                v_.scalar_tensor_tensor(rg[:], hid[:], 0.5, gelu[:], ALU.mult, ALU.mult).then_inc(lru.sem, 1)
                merge(1, 0, True)
                lo(l, P_GL + 9)
                lo(l, P_GL + 11)
                dve.wait_ge(br_hi_done.sem, br_hi_done(l, 5))
                v_.tensor_tensor(br_lo[:, 1], rg[:], br_hi[:, 1].bitcast(F32), ALU.subtract).then_inc(br_ready.sem, 1)
                merge(2, 0, True)
                unit_norm(0, 0)
                lo(l, P_GL + 13)
                unit_norm(1, 0)
                for k in (1, 2):
                    unit_norm(0, k)
                    unit_norm(1, k)
                merge(3, 0, True)
                dve.wait_ge(br_hi_done.sem, br_hi_done(l, 6))
                v_.tensor_tensor(br_lo[:, 0], ret[:].rearrange("p a (k s) -> p (a k) s", s=S), br_hi[:, 0].bitcast(F32), ALU.subtract).then_inc(br_ready.sem, 1)
                def merged_lo(o):
                    dve.wait_ge(m_hi_done.sem, m_hi_done(l, o + 1))
                    rows_of = slice(2 * (o % 2), 2 * (o % 2) + 2)
                    v_.tensor_tensor(br_lo[:, 1 - o // 2, rows_of].rearrange("p k s -> p (k s)"), merged[:, o],
                                     br_hi[:, 1 - o // 2, rows_of].rearrange("p k s -> p (k s)").bitcast(F32), ALU.subtract).then_inc(m_lo_done.sem, 1)

                for j in (1, 2):
                    for v, odd in enumerate(((3, 5), (7,), (9, 11), (13,))):
                        for a in odd:
                            lo(l, P_GL + 12 * j + a)
                        if j == 2 and v == 3:
                            merged_lo(0)
                            merged_lo(1)
                        merge(v, j, False)
                merged_lo(2)
                merged_lo(3)
                for o in range(4):
                    if o < 3:
                        lo(l, P_OUT + 2 * o + 3)
                    dve.wait_ge(used.sem, used(l, P_OUT + 2 * o + 2))
                    z = x_tok[:, :, o * CW:(o + 1) * CW]
                    v_.scalar_tensor_tensor(z, z, ALPHA, bank[o % 2][:, :].rearrange("p (t c) -> p t c", t=T), ALU.mult, ALU.add).then_inc(evac.sem, 1)
                    dve.wait_ge(evac.sem, evac(l, C_OUT + o + 1))
                    for t in range(T):
                        v_.bn_stats(stats[:, t, o], x_tok[:, t, o * CW:(o + 1) * CW]).then_inc(ln.sem, 1)
                norm(l, 0, 4)

                for kk in (0, 2):
                    dve.wait_ge(xt2_ps.sem, xt2_ps(l, kk + 1))
                    v_.tensor_copy(xt[:, 2 * kk:2 * kk + 2].rearrange("p k s -> p (k s)"), bank[4 + kk][:, :]).then_inc(xt2_dve.sem, 1)
                dve.wait_ge(sig_t.sem, sig_t(l, 1))
                dve.wait_ge(par_in.sem, par_in(l, 8 * 16))
                v_.tensor_scalar(sc_t[N_E:2 * N_E, :], sc_t[0:N_E, :], rbl[0:N_E, 0:1], None, ALU.add).then_inc(biased_t.sem, 1)
                dve.wait_ge(sc_tok_ps.sem, sc_tok_ps(l, 1))
                pick_step = seq(route, l)
                v_.tensor_copy(sc[:].rearrange("p t a e -> p (t a e)"), bank[5][:, 0:T * P]).then_inc(route.sem, 1)
                wait_alone(dve, route, l, 1)
                for t in range(T):
                    for e in range(E_GROUPS):
                        v_.max(g8[:, t, e], sc[:, t, 1, e * 8:(e + 1) * 8]).then_inc(route.sem, 1)
                dve.wait_ge(route.sem, route(l, 17))
                pick_step = seq(route, l, 17)
                pick_step(v_.tensor_tensor(grp[:], g8[:, :, :, 0], g8[:, :, :, 1], ALU.add))
                g_flat = grp[:].rearrange("p t g -> p (t g)")
                g_own = g_flat.unsqueeze(2).to_broadcast([P, T * E_GROUPS, E_GROUPS])
                g_all = grp[:].unsqueeze(2).to_broadcast([P, T, E_GROUPS, E_GROUPS])
                c4 = cmp_a[:].rearrange("p (t i) j -> p t i j", t=T)
                d4 = cmp_b[:].rearrange("p (t i) j -> p t i j", t=T)
                o4 = grp[:].unsqueeze(3).to_broadcast([P, T, E_GROUPS, E_GROUPS])
                v_.tensor_tensor(c4, g_all, o4, ALU.is_gt).then_inc(route.sem, 1)
                v_.tensor_tensor(d4, g_all, o4, ALU.is_equal).then_inc(route.sem, 1)
                dve.wait_ge(route.sem, route(l, 20))
                pick_step = seq(route, l, 20)
                lower = tb("lower").unsqueeze(1).to_broadcast([P, T, E_GROUPS * E_GROUPS])
                pick_step(v_.tensor_tensor(cmp_b[:].rearrange("p (t i) j -> p t (i j)", t=T), cmp_b[:].rearrange("p (t i) j -> p t (i j)", t=T), lower, ALU.mult))
                pick_step(v_.tensor_tensor(cmp_a[:], cmp_a[:], cmp_b[:], ALU.add))
                pick_step(v_.tensor_reduce(gpen[:].rearrange("p t g -> p (t g)"), cmp_a[:], AX.X, ALU.add))
                pick_step(v_.tensor_scalar(gmask[:], gpen[:], float(TOP_GROUPS), None, ALU.is_lt))
                pick_step(v_.tensor_scalar(gpen[:], gmask[:], 1.0, BIG, ALU.subtract, ALU.mult))
                m4 = masked[:].rearrange("p t (g e) -> p t g e", g=E_GROUPS)
                biased4 = sc[:, :, 1].rearrange("p t (g e) -> p t g e", g=E_GROUPS)
                pick_step(v_.tensor_tensor(m4, biased4, gmask[:].unsqueeze(3).to_broadcast([P, T, E_GROUPS, 8]), ALU.mult))
                v_.tensor_tensor(m4, m4, gpen[:].unsqueeze(3).to_broadcast([P, T, E_GROUPS, 8]), ALU.add).then_inc(route.sem, 1)
                wait_alone(dve, route, l, 27)
                for t in range(T):
                    v_.max(best[:, t], masked[:, t]).then_inc(route.sem, 1)
                wait_alone(dve, route, l, 29)
                for t in range(T):
                    v_.match_replace(taken[:, t], best[:, t], masked[:, t], -3 * BIG).then_inc(route.sem, 1)
                dve.wait_ge(route.sem, route(l, 31))
                v_.tensor_tensor(chosen[:], masked[:], taken[:], ALU.not_equal).then_inc(route.sem, 1)
                dve.wait_ge(route.sem, route(l, 32))
                v_.tensor_tensor(weight[:], chosen[:], sc[:, :, 0], ALU.mult).then_inc(route.sem, 1)
                dve.wait_ge(route.sem, route(l, 33))
                pick_step = seq(route, l, 33)
                pick_step(v_.tensor_reduce(den[:], weight[:], AX.X, ALU.add))
                pick_step(v_.reciprocal(den[:], den[:]))
                for t in range(T):
                    v_.tensor_scalar(weight[:, t], weight[:, t], den[:, t:t + 1], ROUTED_SCALE, ALU.mult, ALU.mult).then_inc(route.sem, 1)
                dve.wait_ge(rank_ps.sem, rank_ps(l, 1))
                ranks = bank[4][:, 0:2 * N_E].rearrange("p (t e) -> p t e", t=T)
                v_.scalar_tensor_tensor(rank[:, :, 0:N_E], chosen[:], FAR, ranks, ALU.mult, ALU.add).then_inc(route.sem, 1)
                v_.tensor_reduce(most[:], bank[4][:, 2 * N_E:3 * N_E], AX.X, ALU.max).then_inc(route.sem, 1)
                dve.wait_ge(route.sem, route(l, 39))
                for r in range(1, MAX_ROUNDS):
                    v_.tensor_scalar(rank[:, :, r * N_E:(r + 1) * N_E], rank[:, :, 0:N_E], float(CAP * r), None, ALU.subtract).then_inc(route.sem, 1)
                v_.memset(rank[:, :, MAX_ROUNDS * N_E:], 0.0).then_inc(route.sem, 1)
                v_.tensor_scalar(over[:, 0:MAX_ROUNDS - 1], tb("thresh"), most[:, 0:1], None, ALU.is_lt).then_inc(route.sem, 1)
                dve.wait_ge(route.sem, route(l, 44))
                v_.tensor_reduce(most[:], over[:, 0:MAX_ROUNDS - 1], AX.X, ALU.add).then_inc(route.sem, 1)
                dve.wait_ge(route.sem, route(l, 45))
                v_.tensor_scalar(rounds_i[:], most[:], 1.0, None, ALU.add).then_inc(rounds_ready.sem, 1)

                def build_pick(n):
                    r4 = rank[:].rearrange("p t (q e) -> p t q e", e=QUAD)
                    for t in range(T):
                        ins = v_.tensor_tensor(pick[:, t], tb("slot").unsqueeze(1).to_broadcast([P, QUAD, CAP]),
                                               r4[:, t, n].unsqueeze(2).to_broadcast([P, QUAD, CAP]), ALU.is_equal)
                    ins.then_inc(picked, 1)

                build_pick(0)
                dve.wait_ge(sh_sg.sem, sh_sg(l, 1))
                v_.tensor_tensor(shared_t, bank[6][:, :], shared_sg, ALU.mult).then_inc(sh_h.sem, 1)
                dve.wait_ge(sh_ps.sem, sh_ps(l, 2))
                dve.wait_ge(sh_h.sem, sh_h(l, 1))
                v_.tensor_tensor(shared_h[:], bank[7][:, :].rearrange("p (j s) -> p j s", j=2), shared_t.rearrange("p (j s) -> p j s", j=2), ALU.mult).then_inc(sh_h.sem, 1)
                wait_alone(dve, rounds_ready, l, 1)
                rounds = dve.value_load(rounds_i[0:1, 0:1], min_val=1, max_val=MAX_ROUNDS)
                q_first = dve.snap(quads)
                with dve.Fori(0, rounds * NQ) as n:
                    q = q_first + n
                    for g in (0, 2):
                        dve.wait_ge(gathered, 4 * q + g + 1)
                        v_.tensor_copy(xg[:, 2 * g:2 * g + 2].rearrange("p k s -> p (k s)"), bank[4][:, :]).then_inc(xg_dve, 1)
                    dve.wait_ge(gathered, 4 * q + 4)
                    dve.wait_ge(picked_w, q + 1)
                    build_pick(n + 1)

                    def hidden(X):
                        dve.wait_ge(h_sg, 2 * q + X + 1)
                        v_.tensor_tensor(m_t[:, X], bank[6 + X][:, 0:FE], m_sg[:, X], ALU.mult).then_inc(h_t, 1)
                        dve.wait_ge(h_t, 2 * q + X + 1)
                        v_.tensor_tensor(m_h[:, X].rearrange("p j q -> p q j"), bank[6 + X][:, FE:2 * FE].rearrange("p (q j) -> p q j", j=2),
                                         m_t[:, X].rearrange("p (q j) -> p q j", j=2), ALU.mult).then_inc(h_done, 1)

                    hidden(0)
                    dve.wait_ge(pick_t_ps, q + 2)
                    v_.tensor_scalar(pick_t[:].rearrange("p a s -> p (a s)"), bank[4][:, :], 0.0, None, ALU.is_gt).then_inc(pick_t_done, 1)
                    v_.tensor_reduce(slot_gate[:], bank[4][:, :].rearrange("p (a s) -> p a s", a=2), AX.X, ALU.add).then_inc(pick_t_done, 1)
                    hidden(1)
                    for X in range(2):
                        for half in range(2):
                            dve.wait_ge(y_hi_done, 4 * q + 2 * X + half + 1)
                            v_.scalar_tensor_tensor(y_lo[:, half], bank[6 + half][:, :], slot_gate[:, X:X + 1], y_hi[:, half].bitcast(F32),
                                                    ALU.mult, ALU.subtract).then_inc(y_lo_done, 1)
                dve.reg_add(quads, quads, rounds * NQ)
                all_quads = dve.snap(quads)
                for half in range(2):
                    dve.wait_ge(added[half], all_quads)
                    for t in range(T):
                        z = x_tok[:, t, half * 512:(half + 1) * 512]
                        ins = v_.scalar_tensor_tensor(z, z, ALPHA, bank[2 * t + half][:, :], ALU.mult, ALU.add)
                    ins.then_inc(route.sem, 1)
                    dve.wait_ge(route.sem, route(l, 46 + half))
                    for t in range(T):
                        v_.bn_stats(stats[:, t, half], x_tok[:, t, half * 512:(half + 1) * 512]).then_inc(ln.sem, 1)
                norm(l, 1, 2)


def kernel(**inputs):
    import numpy as _np
    import concourse.bacc as _bacc
    from concourse import mybir as _mybir
    from concourse.bass_utils import run_bass_kernel_spmd as _run

    nc = _bacc.Bacc("TRN2", target_bir_lowering=False, num_devices=1)
    arrays, args = {}, {}
    for name in _INS:
        a = shape_tables() if name == "tables" else _np.ascontiguousarray(inputs[name])
        arrays[f"in_{name}_dram"] = a
        args[name] = nc.dram_tensor(f"in_{name}_dram", a.shape, _mybir.dt.from_np(a.dtype), kind="ExternalInput").ap()
    out = nc.dram_tensor("out_dram", [1, S, D], F32, kind="ExternalOutput").ap()
    trunk(nc, out=out, **args)
    return _run(nc, [arrays], core_ids=[0]).results[0]["out_dram"]


_INS = ("x", "positions", "tables", "w_in", "gate_b", "w_branch", "w_out", "pool_w", "pool_scale", "rg_conv_w",
        "rg_conv_b", "rg_wa", "rg_ba", "rg_wx", "rg_bx", "rg_lambda", "ln1_g", "ln1_b", "router_w", "router_bias",
        "exp_w1", "exp_w3", "exp_w2", "sh_w1", "sh_w3", "sh_w2", "ln2_g", "ln2_b")
```
